# Optimizing a Trainium2 kernel written in Bass

```python
import math
import jax, jax.numpy as jnp
from jax import lax
import numpy as np

D_MODEL = 1024
BATCH = 1
SEQ = 512
DEPTH = 1

MIX_WIDTH = D_MODEL
DN_HEADS = 4
DN_HEAD_DIM = MIX_WIDTH // 2 // DN_HEADS
DN_WIDTH = DN_HEADS * DN_HEAD_DIM
CONV_WIDTH = 4
CHUNK = 64
POOL_WINDOWS = (2, 4, 8, 16)
POOL_GROUPS = len(POOL_WINDOWS)
POOL_WIDTH = MIX_WIDTH - DN_WIDTH
POOL_GROUP_DIM = POOL_WIDTH // POOL_GROUPS
IN_WIDTH = 4 * DN_WIDTH + 2 * DN_HEADS + POOL_WIDTH
PEER_HEADS = 8
N_KEYS = 128
N_EXPERTS = N_KEYS * N_KEYS
PEER_QUERY_DIM = 256
PEER_HALF = PEER_QUERY_DIM // 2
PEER_TOPK = 16
PEER_TOKEN_BLOCK = 128
EPS = 1e-6


def _rmsnorm(x, w):
    xf = x.astype(jnp.float32)
    y = xf * lax.rsqrt(jnp.mean(xf * xf, axis=-1, keepdims=True) + EPS)
    return (y * w.astype(jnp.float32)).astype(x.dtype)

def _l2norm(x):
    return x * lax.rsqrt(jnp.sum(x * x, axis=-1, keepdims=True) + EPS)

def _causal_conv(x, w):
    c = x.shape[-1]
    return lax.conv_general_dilated(
        x, w[:, None, :].astype(x.dtype), window_strides=(1,),
        padding=((CONV_WIDTH - 1, 0),),
        dimension_numbers=("NWC", "WIO", "NWC"), feature_group_count=c)

def _chunk_gated_delta_rule(q, k, v, g, beta):
    b, s, h, dk = q.shape
    dv = v.shape[-1]
    n = s // CHUNK
    q = q * (dk ** -0.5)

    def to_chunks(t):
        return t.reshape(b, n, CHUNK, h, -1).transpose(0, 3, 1, 2, 4)

    q, k, v = to_chunks(q), to_chunks(k), to_chunks(v)
    g = g.reshape(b, n, CHUNK, h).transpose(0, 3, 1, 2)
    beta = beta.reshape(b, n, CHUNK, h).transpose(0, 3, 1, 2)
    g = jnp.cumsum(g, axis=-1)
    k_beta = k * beta[..., None]
    v_beta = v * beta[..., None]
    causal = jnp.tril(jnp.ones((CHUNK, CHUNK), dtype=bool))
    strict = jnp.tril(jnp.ones((CHUNK, CHUNK), dtype=bool), -1)
    decay = jnp.exp(jnp.where(causal, g[..., :, None] - g[..., None, :], -jnp.inf))
    a_mat = jnp.where(strict, jnp.einsum("bhnid,bhnjd->bhnij", k_beta, k) * decay, 0.0)
    eye = jnp.eye(CHUNK, dtype=q.dtype)
    t_mat = lax.linalg.triangular_solve(eye + a_mat, jnp.broadcast_to(eye, a_mat.shape),
                                        left_side=True, lower=True)
    w_vals = jnp.einsum("bhnij,bhnjd->bhnid", t_mat, v_beta)
    k_cumdecay = jnp.einsum("bhnij,bhnjd->bhnid", t_mat, k_beta * jnp.exp(g)[..., None])
    attn_intra = jnp.where(causal, jnp.einsum("bhnid,bhnjd->bhnij", q, k) * decay, 0.0)
    g_last = g[..., -1]
    k_decay = k * jnp.exp(g_last[..., None] - g)[..., None]
    q_decay = q * jnp.exp(g)[..., None]
    xs = (jnp.moveaxis(q_decay, 2, 0), jnp.moveaxis(k_cumdecay, 2, 0), jnp.moveaxis(w_vals, 2, 0),
          jnp.moveaxis(attn_intra, 2, 0), jnp.moveaxis(k_decay, 2, 0), jnp.moveaxis(g_last, 2, 0))

    def step(state, inp):
        qd, kcd, wv, attn_c, kd, gl = inp
        v_new = wv - jnp.einsum("bhcd,bhde->bhce", kcd, state)
        o = jnp.einsum("bhcd,bhde->bhce", qd, state) + jnp.einsum("bhij,bhje->bhie", attn_c, v_new)
        state = state * jnp.exp(gl)[..., None, None] + jnp.einsum("bhcd,bhce->bhde", kd, v_new)
        return state, o

    state0 = jnp.zeros((b, h, dk, dv), dtype=q.dtype)
    _, o = lax.scan(step, state0, xs)
    return o.transpose(1, 0, 3, 2, 4).reshape(b, s, h, dv)

def _multiscale_pool(p, w_pool, pool_scale):
    b, s, _ = p.shape
    pf = p.astype(jnp.float32).reshape(b, s, POOL_GROUPS, POOL_GROUP_DIM)
    cs = jnp.cumsum(pf, axis=1)
    pos = jnp.arange(1, s + 1, dtype=jnp.int32)
    outs = []
    for gi, w in enumerate(POOL_WINDOWS):
        c = cs[:, :, gi]
        lower = jnp.pad(c, ((0, 0), (w, 0), (0, 0)))[:, :s]
        count = jnp.minimum(pos, w).astype(jnp.float32)[None, :, None]
        outs.append((c - lower) / count - pf[:, :, gi])
    pooled = jnp.stack(outs, axis=2)
    mixed = jnp.einsum("bsgc,gcd->bsgd", pooled, w_pool.astype(jnp.float32))
    return mixed.reshape(b, s, POOL_WIDTH) * pool_scale.astype(jnp.float32)

def _peer(xn, w_query, sub_keys, expert_down, expert_up):
    b, s, d = xn.shape
    blocks = xn.reshape(-1, PEER_TOKEN_BLOCK, d)
    sk = sub_keys.astype(jnp.float32)

    def block(xb):
        t = xb.shape[0]
        q = (xb @ w_query).astype(jnp.float32).reshape(t, PEER_HEADS, 2, PEER_HALF)
        scores = jnp.einsum("thpc,hpkc->thpk", q, sk)
        s1, i1 = lax.top_k(scores[:, :, 0], PEER_TOPK)
        s2, i2 = lax.top_k(scores[:, :, 1], PEER_TOPK)
        cand = (s1[..., :, None] + s2[..., None, :]).reshape(t, PEER_HEADS, PEER_TOPK * PEER_TOPK)
        cand_idx = (i1[..., :, None] * N_KEYS + i2[..., None, :]).reshape(t, PEER_HEADS, PEER_TOPK * PEER_TOPK)
        top_s, top_pos = lax.top_k(cand, PEER_TOPK)
        idx = jnp.take_along_axis(cand_idx, top_pos, axis=-1)
        gate = jax.nn.softmax(top_s, axis=-1)
        u = expert_down[idx]
        v = expert_up[idx]
        act = jax.nn.gelu(jnp.einsum("td,thkd->thk", xb, u).astype(jnp.float32), approximate=False)
        return jnp.einsum("thk,thkd->td", (gate * act).astype(v.dtype), v)

    return lax.map(block, blocks).reshape(b, s, d).astype(xn.dtype)

def first_inputs(seed: int = 0) -> dict:
    key = jax.random.key(seed)
    ks = jax.random.split(key, 16)
    f32 = jnp.float32
    L = DEPTH

    def gain(k, shape):
        return 1.0 + 0.02 * jax.random.normal(k, shape, f32)

    x = jax.random.normal(ks[0], (BATCH, SEQ, D_MODEL), f32)
    norm_mix_w = gain(ks[1], (L, D_MODEL))
    w_in = jax.random.normal(ks[2], (L, D_MODEL, IN_WIDTH), f32) * D_MODEL ** -0.5
    conv_w = jax.random.normal(ks[3], (L, CONV_WIDTH, 3 * DN_WIDTH), f32) * CONV_WIDTH ** -0.5
    a_log = jnp.log(jax.random.uniform(ks[4], (L, DN_HEADS), f32, 1.0, 16.0))
    dt = jnp.exp(jax.random.uniform(ks[5], (L, DN_HEADS), f32, math.log(1e-3), math.log(1e-1)))
    dt_bias = dt + jnp.log(-jnp.expm1(-dt))
    dn_norm_w = gain(ks[6], (L, DN_HEAD_DIM))
    w_pool = jax.random.normal(ks[7], (L, POOL_GROUPS, POOL_GROUP_DIM, POOL_GROUP_DIM), f32) * POOL_GROUP_DIM ** -0.5
    pool_scale = gain(ks[8], (L, POOL_WIDTH))
    w_out = jax.random.normal(ks[9], (L, MIX_WIDTH, D_MODEL), f32) * MIX_WIDTH ** -0.5
    norm_ffn_w = gain(ks[10], (L, D_MODEL))
    w_query = jax.random.normal(ks[11], (L, D_MODEL, PEER_HEADS * PEER_QUERY_DIM), f32) * D_MODEL ** -0.5
    sub_keys = jax.random.normal(ks[12], (L, PEER_HEADS, 2, N_KEYS, PEER_HALF), f32) * PEER_HALF ** -0.5
    expert_down = jax.random.normal(ks[13], (L, N_EXPERTS, D_MODEL), f32) * D_MODEL ** -0.5
    expert_up = jax.random.normal(ks[14], (L, N_EXPERTS, D_MODEL), f32) * PEER_HEADS ** -0.5
    norm_final_w = gain(ks[15], (D_MODEL,))
    return {"x": x, "norm_mix_w": norm_mix_w, "w_in": w_in, "conv_w": conv_w, "a_log": a_log,
            "dt_bias": dt_bias, "dn_norm_w": dn_norm_w, "w_pool": w_pool, "pool_scale": pool_scale,
            "w_out": w_out, "norm_ffn_w": norm_ffn_w, "w_query": w_query, "sub_keys": sub_keys,
            "expert_down": expert_down, "expert_up": expert_up, "norm_final_w": norm_final_w}

def first_block(x, norm_mix_w, w_in, conv_w, a_log, dt_bias, dn_norm_w, w_pool, pool_scale,
              w_out, norm_ffn_w, w_query, sub_keys, expert_down, expert_up, norm_final_w):
    b, s, _ = x.shape
    for l in range(DEPTH):
        h = _rmsnorm(x, norm_mix_w[l])
        proj = h @ w_in[l]
        qkv = proj[..., :3 * DN_WIDTH]
        z = proj[..., 3 * DN_WIDTH:4 * DN_WIDTH]
        b_gate = proj[..., 4 * DN_WIDTH:4 * DN_WIDTH + DN_HEADS]
        a_dec = proj[..., 4 * DN_WIDTH + DN_HEADS:4 * DN_WIDTH + 2 * DN_HEADS]
        p = proj[..., 4 * DN_WIDTH + 2 * DN_HEADS:]
        qkv = jax.nn.silu(_causal_conv(qkv, conv_w[l])).astype(jnp.float32)
        q = _l2norm(qkv[..., :DN_WIDTH].reshape(b, s, DN_HEADS, DN_HEAD_DIM))
        k = _l2norm(qkv[..., DN_WIDTH:2 * DN_WIDTH].reshape(b, s, DN_HEADS, DN_HEAD_DIM))
        v = qkv[..., 2 * DN_WIDTH:].reshape(b, s, DN_HEADS, DN_HEAD_DIM)
        beta = jax.nn.sigmoid(b_gate.astype(jnp.float32))
        g = -jnp.exp(a_log[l].astype(jnp.float32)) * jax.nn.softplus(
            a_dec.astype(jnp.float32) + dt_bias[l].astype(jnp.float32))
        o = _chunk_gated_delta_rule(q, k, v, g, beta)
        o = _rmsnorm(o, dn_norm_w[l]) * jax.nn.silu(
            z.astype(jnp.float32).reshape(b, s, DN_HEADS, DN_HEAD_DIM))
        o = o.reshape(b, s, DN_WIDTH).astype(x.dtype)
        pool_out = _multiscale_pool(p, w_pool[l], pool_scale[l]).astype(x.dtype)
        x = x + jnp.concatenate([o, pool_out], axis=-1) @ w_out[l]
        x = x + _peer(_rmsnorm(x, norm_ffn_w[l]), w_query[l], sub_keys[l], expert_down[l], expert_up[l])
    return _rmsnorm(x, norm_final_w)


N_MIXERS = 4
N_HEADS = 16
HEAD_DIM = D_MODEL // N_HEADS
SB_BLOCK = 128
GMLP_BLOCK = 128
GMLP_WIDTH = 2 * D_MODEL
GMLP_GROUPS = 8
CONV_WIDTH_2 = 3
BAND_CHUNKS = 8
REL_CLIP = 128
D_FF = -(-8 * D_MODEL // (3 * 256)) * 256


def rms_norm(x, g):
    xf = x.astype(jnp.float32)
    y = xf * lax.rsqrt(jnp.mean(xf * xf, axis=-1, keepdims=True) + EPS)
    return (y * g.astype(jnp.float32)).astype(x.dtype)

def layer_norm(x, g):
    xf = x.astype(jnp.float32)
    mu = jnp.mean(xf, axis=-1, keepdims=True)
    xc = xf - mu
    var = jnp.mean(xc * xc, axis=-1, keepdims=True)
    return (xc * lax.rsqrt(var + EPS) * g.astype(jnp.float32)).astype(x.dtype)

def modulate(h, shift, scale):
    return h * (1 + scale) + shift

def stick_breaking_mixer(h, w_qkv, w_o):
    b, s, _ = h.shape
    qkv = (h @ w_qkv).reshape(b, s, 3, N_HEADS, HEAD_DIM)
    q, k, v = qkv[:, :, 0], qkv[:, :, 1], qkv[:, :, 2]
    scale = HEAD_DIM ** -0.5
    outs = []
    for q0 in range(0, s, SB_BLOCK):
        end = q0 + SB_BLOCK
        z = jnp.einsum('bthd,bshd->bhts', q[:, q0:end], k[:, :end]).astype(jnp.float32) * scale
        t_pos = q0 + jnp.arange(SB_BLOCK)[:, None]
        s_pos = jnp.arange(end)[None, :]
        mask = s_pos < t_pos
        sp = jnp.where(mask, jax.nn.softplus(z), 0.0)
        rest = lax.cumsum(sp, axis=3, reverse=True)
        log_a = jnp.where(mask, z - rest, -jnp.inf)
        a = jnp.exp(log_a).astype(v.dtype)
        outs.append(jnp.einsum('bhts,bshd->bthd', a, v[:, :end]))
    o = jnp.concatenate(outs, axis=1).reshape(b, s, D_MODEL)
    return o @ w_o

def spatial_gating_mixer(h, w_in, ln_g, w_s, s_bias, w_out):
    b, s, _ = h.shape
    z = jax.nn.gelu(h @ w_in)
    u, v = jnp.split(z, 2, axis=-1)
    v = layer_norm(v, ln_g)
    nb = s // GMLP_BLOCK
    gc = GMLP_WIDTH // GMLP_GROUPS
    v = v.reshape(b, nb, GMLP_BLOCK, GMLP_GROUPS, gc)
    pos_chunk = jnp.arange(GMLP_BLOCK) // CHUNK
    mask = pos_chunk[:, None] >= pos_chunk[None, :]
    ws = jnp.where(mask[None], w_s, 0.0).astype(v.dtype)
    sv = jnp.einsum('gij,bnjgc->bnigc', ws, v) + s_bias.T[:, :, None].astype(v.dtype)
    y = u * sv.reshape(b, s, GMLP_WIDTH)
    return y @ w_out

def short_conv_mixer(h, w_in, conv_w, w_out):
    gb, gc, xt = jnp.split(h @ w_in, 3, axis=-1)
    y = gc * xt
    yc = lax.conv_general_dilated(
        y, conv_w.reshape(CONV_WIDTH_2, 1, D_MODEL).astype(y.dtype),
        window_strides=(1,), padding=[(CONV_WIDTH_2 - 1, 0)],
        dimension_numbers=('NWC', 'WIO', 'NWC'), feature_group_count=D_MODEL)
    return (gb * yc) @ w_out

def chunk_band_attention_mixer(h, w_qkv, rel_bias, w_o):
    b, s, _ = h.shape
    nc = s // CHUNK
    nband = BAND_CHUNKS + 1
    qkv = (h @ w_qkv).reshape(b, s, 3, N_HEADS, HEAD_DIM)
    q = qkv[:, :, 0].reshape(b, nc, CHUNK, N_HEADS, HEAD_DIM)
    pad = ((0, 0), (BAND_CHUNKS * CHUNK, 0), (0, 0), (0, 0))
    kp = jnp.pad(qkv[:, :, 1], pad).reshape(b, nc + BAND_CHUNKS, CHUNK, N_HEADS, HEAD_DIM)
    vp = jnp.pad(qkv[:, :, 2], pad).reshape(b, nc + BAND_CHUNKS, CHUNK, N_HEADS, HEAD_DIM)
    scale = HEAD_DIM ** -0.5
    scores = jnp.concatenate(
        [jnp.einsum('bcihd,bcjhd->bhcij', q, kp[:, o:o + nc]) for o in range(nband)],
        axis=-1).astype(jnp.float32) * scale
    i_pos = jnp.arange(CHUNK)[:, None]
    j_pos = jnp.arange(nband * CHUNK)[None, :]
    dist = i_pos + BAND_CHUNKS * CHUNK - j_pos
    idx = jnp.clip(dist, -REL_CLIP, REL_CLIP) + REL_CLIP
    bias = rel_bias[:, idx].astype(jnp.float32)
    key_chunk = jnp.arange(nc)[:, None] - BAND_CHUNKS + j_pos // CHUNK
    valid = (key_chunk >= 0)[:, None, :]
    scores = jnp.where(valid, scores + bias[:, None], -jnp.inf)
    p = jax.nn.softmax(scores, axis=-1).astype(vp.dtype)
    out = jnp.einsum('bhcij,bcjhd->bcihd', p[..., :CHUNK], vp[:, 0:nc])
    for o in range(1, nband):
        out = out + jnp.einsum('bhcij,bcjhd->bcihd', p[..., o * CHUNK:(o + 1) * CHUNK], vp[:, o:o + nc])
    return out.reshape(b, s, D_MODEL) @ w_o

def swiglu_ffn(h, w_in, w_out):
    g, u = jnp.split(h @ w_in, 2, axis=-1)
    return (jax.nn.silu(g) * u) @ w_out

def _n_layers_of(m):
    return len(range(m, DEPTH, N_MIXERS))

def _dense(key, shape, fan_in, gain=1.0):
    return jax.random.normal(key, shape, jnp.float32) * (gain * fan_in ** -0.5)

def second_inputs(seed: int = 0) -> dict:
    key = jax.random.key(seed)
    ks = jax.random.split(key, 21)
    na, nb, ncv, nd = (_n_layers_of(m) for m in range(N_MIXERS))
    D = D_MODEL
    nrm = lambda k, shape: jax.random.normal(k, shape, jnp.float32)
    return {
        "x": nrm(ks[0], (BATCH, SEQ, D)),
        "c": nrm(ks[1], (BATCH, D)),
        "ada_w": _dense(ks[2], (DEPTH, D, 6 * D), D, 0.5),
        "ada_b": 0.02 * nrm(ks[3], (DEPTH, 6 * D)),
        "norm_g": 1.0 + 0.1 * nrm(ks[4], (DEPTH, 4, D)),
        "ffn_w_in": _dense(ks[5], (DEPTH, D, 2 * D_FF), D),
        "ffn_w_out": _dense(ks[6], (DEPTH, D_FF, D), D_FF),
        "sb_w_qkv": _dense(ks[7], (na, D, 3 * D), D),
        "sb_w_o": _dense(ks[8], (na, D, D), D),
        "sg_w_in": _dense(ks[9], (nb, D, 2 * GMLP_WIDTH), D),
        "sg_ln_g": 1.0 + 0.1 * nrm(ks[10], (nb, GMLP_WIDTH)),
        "sg_w_s": _dense(ks[11], (nb, GMLP_GROUPS, GMLP_BLOCK, GMLP_BLOCK), GMLP_BLOCK),
        "sg_bias": 1.0 + 0.1 * nrm(ks[12], (nb, GMLP_GROUPS, GMLP_BLOCK)),
        "sg_w_out": _dense(ks[13], (nb, GMLP_WIDTH, D), GMLP_WIDTH),
        "sc_w_in": _dense(ks[14], (ncv, D, 3 * D), D),
        "sc_conv_w": _dense(ks[15], (ncv, CONV_WIDTH_2, D), CONV_WIDTH_2),
        "sc_w_out": _dense(ks[16], (ncv, D, D), D),
        "cb_w_qkv": _dense(ks[17], (nd, D, 3 * D), D),
        "cb_rel_bias": 0.5 * nrm(ks[18], (nd, N_HEADS, 2 * REL_CLIP + 1)),
        "cb_w_o": _dense(ks[19], (nd, D, D), D),
    }

def second_block(x, c, ada_w, ada_b, norm_g, ffn_w_in, ffn_w_out,
              sb_w_qkv, sb_w_o,
              sg_w_in, sg_ln_g, sg_w_s, sg_bias, sg_w_out,
              sc_w_in, sc_conv_w, sc_w_out,
              cb_w_qkv, cb_rel_bias, cb_w_o):
    mod_all = jnp.einsum('bd,lde->lbe', jax.nn.silu(c), ada_w) + ada_b[:, None]
    for i in range(DEPTH):
        m, r = i % N_MIXERS, i // N_MIXERS
        sh_m, sc_m, gt_m, sh_f, sc_f, gt_f = jnp.split(mod_all[i][:, None, :], 6, axis=-1)
        h = modulate(rms_norm(x, norm_g[i, 0]), sh_m, sc_m)
        if m == 0:
            y = stick_breaking_mixer(h, sb_w_qkv[r], sb_w_o[r])
        elif m == 1:
            y = spatial_gating_mixer(h, sg_w_in[r], sg_ln_g[r], sg_w_s[r], sg_bias[r], sg_w_out[r])
        elif m == 2:
            y = short_conv_mixer(h, sc_w_in[r], sc_conv_w[r], sc_w_out[r])
        else:
            y = chunk_band_attention_mixer(h, cb_w_qkv[r], cb_rel_bias[r], cb_w_o[r])
        x = x + gt_m * rms_norm(y, norm_g[i, 1])
        h = modulate(rms_norm(x, norm_g[i, 2]), sh_f, sc_f)
        y = swiglu_ffn(h, ffn_w_in[i], ffn_w_out[i])
        x = x + gt_f * rms_norm(y, norm_g[i, 3])
    return x


def setup_inputs(seed=0):
    out = dict(first_inputs(seed))
    for name, value in second_inputs(seed + 1).items():
        if name != "x":
            out[name + "_2"] = value
    return out


def reference(
    x, norm_mix_w, w_in, conv_w, a_log, dt_bias, dn_norm_w, w_pool, pool_scale, w_out,
    norm_ffn_w, w_query, sub_keys, expert_down, expert_up, norm_final_w, c_2, ada_w_2, ada_b_2,
    norm_g_2, ffn_w_in_2, ffn_w_out_2, sb_w_qkv_2, sb_w_o_2, sg_w_in_2, sg_ln_g_2, sg_w_s_2,
    sg_bias_2, sg_w_out_2, sc_w_in_2, sc_conv_w_2, sc_w_out_2, cb_w_qkv_2, cb_rel_bias_2,
    cb_w_o_2,
):
    x = first_block(
        x, norm_mix_w, w_in, conv_w, a_log, dt_bias, dn_norm_w, w_pool, pool_scale, w_out,
        norm_ffn_w, w_query, sub_keys, expert_down, expert_up, norm_final_w,
    )
    return second_block(
        x, c_2, ada_w_2, ada_b_2, norm_g_2, ffn_w_in_2, ffn_w_out_2, sb_w_qkv_2, sb_w_o_2,
        sg_w_in_2, sg_ln_g_2, sg_w_s_2, sg_bias_2, sg_w_out_2, sc_w_in_2, sc_conv_w_2,
        sc_w_out_2, cb_w_qkv_2, cb_rel_bias_2, cb_w_o_2,
    )


_drawn_inputs = setup_inputs


def setup_inputs(seed=0):
    import zlib

    import numpy as np

    out = dict(_drawn_inputs(seed))
    spreads = {}
    factors = {'dn_norm_w': 48.773,
     'pool_scale': 34.355,
     'norm_final_w': 22.349,
     'norm_ffn_w': 19.918,
     'ada_b_2': 13.255,
     'norm_g_2': 6.059}
    for name, (base, spread) in spreads.items():
        noise = np.random.default_rng([zlib.crc32(name.encode()), seed]).standard_normal(out[name].shape)
        drawn = base * np.exp(spread * noise) if base else spread * noise
        out[name] = __import__('jax').numpy.asarray(drawn.astype(out[name].dtype))
    for name, factor in factors.items():
        out[name] = (out[name] * factor).astype(out[name].dtype)
    return out
```

```python
from contextlib import ExitStack

import numpy as np
import concourse.bass as bass
from concourse import mybir

F32 = mybir.dt.float32
F32R = mybir.dt.float32r
U32 = mybir.dt.uint32
ALU = mybir.AluOpType
ACT = mybir.ActivationFunctionType
AX = mybir.AxisListType

P = 128
D = 1024
S = 512
T = S // P
KD = D // P
H = 4
CW = 4
POOLS = (2, 4, 8, 16)
QKV = 3 * H
PH = 8
NK = 128
TOPK = 16
EXPERTS = NK * NK
AH = 16
FF = 2816
FT = FF // P
EPS = 1e-6
HALF = 512

N_IN = 5
N_OUT = 2
N_QUERY = 4
EARLY = N_IN + N_OUT + N_QUERY
OUT0 = N_IN
QUERY0 = OUT0 + N_OUT
N_QKV2 = 6
N_O2 = 2
N_FIN = FT // 2
N_FOUT = -(-FT // 4)
LATE = N_QKV2 + N_O2 + N_FIN + N_FOUT
FIN0 = N_QKV2 + N_O2
FOUT0 = FIN0 + N_FIN
UNIT_O2 = 4 * N_QKV2
UNIT_FIN = UNIT_O2 + 4 * N_O2
UNIT_FOUT = UNIT_FIN + 4 * N_FIN
UNITS = UNIT_FOUT + FT
N_MODC = 8
N_GATE = 4

C_IDENT, C_UI, C_ONES, C_US, C_LS, C_NLOW, C_NONE, C_NEG = range(8)
LEVELS = 7
GRING = 8
BATCH = 4


def offsets(**sizes):
    at, out = 0, {}
    for name, n in sizes.items():
        out[name] = (at, n)
        at += n
    return out, at


VEC, NVEC = offsets(norm_mix=KD, conv=QKV * CW, dn=1, pool=T, g0=KD, g2=KD, c=KD, ada=4 * KD, alog=H, dtb=H)


def shape_constants():
    i = np.arange(P)
    r, c = i[:, None], i[None, :]
    mats = [r == c, r <= c, np.ones((P, P)), r < c, r > c, -1.0 * (r >= c), -np.ones((P, P)), -1e30 * (r >= c)]
    corr = np.ones((len(POOLS), 16), np.float32)
    for g, w in enumerate(POOLS):
        t = np.arange(16)
        corr[g] = np.where(t < w, w / (np.minimum(t, w - 1) + 1.0), 1.0)
    flat = [np.asarray(m, np.float32) for m in mats]
    flat += [np.tile(np.arange(16, dtype=np.float32), (P, 1)), np.tile(corr.reshape(1, -1), (P, 1))]
    consts = np.concatenate(flat, axis=1).astype(np.float32)
    levels = []
    for n in range(LEVELS):
        b = 1 << n
        levels.append((r // (2 * b) == c // (2 * b)) & (r // b % 2 == 1) & (c // b % 2 == 0))
    return consts, np.concatenate(levels, axis=1).astype(np.float32)


class Own:

    def __init__(self, eng, sem):
        self.eng, self.sem, self.n = eng, sem, 0

    def step(self, ins):
        ins.then_inc(self.sem, 1)
        self.n += 1
        self.eng.wait_ge(self.sem, self.n)


def block_kernel(nc, a, out):
    ctx = ExitStack()
    with ctx:
        def sb(name, shape, dt=F32):
            return ctx.enter_context(nc.sbuf_tensor(name, shape, dt))

        def sem(name):
            return ctx.enter_context(nc.semaphore(name))

        x = sb("x", [P, T, D])
        consts = sb("consts", [P, 8 * P + 16 + 64])
        vecs = sb("vecs", [P, NVEC])
        gtrow = sb("gtrow", [P, 2, D])
        modc = sb("modc", [P, 4, KD])
        with nc.sbuf_tensor("r_low", [P, 48 * 256], F32R) as r_low, nc.sbuf_tensor("middle", [P, 36 * 256], F32) as middle, \
                nc.sbuf_tensor("r_high", [P, 88 * 256], F32R) as r_high:
            pass
        with nc.sbuf_tensor("below", [P, 128 * 256], F32), nc.sbuf_tensor("upper", [P, 44 * 256], F32) as upper:
            pass
        arena = sb("arena", [P, 172 * 256])
        stat = sb("stat", [P, 16, T])
        gates = sb("gates", [P, 16, T * H])
        ccol = sb("ccol", [P, KD])
        ealog = sb("ealog", [P, H])
        wba = sb("wba", [P, KD, 2 * H])
        sel = sb("sel", [P, 1200])
        selu = sb("selu", [P, 160], U32)
        ps = ctx.enter_context(nc.psum_tensor("ps", [P, 8, HALF], F32))
        psf = ps[:, :, :].rearrange("p b n -> p (b n)")

        def const(n):
            return consts[:, n * P:(n + 1) * P]

        iota16 = consts[:, 8 * P:8 * P + 16]
        corr = consts[:, 8 * P + 16:8 * P + 80].rearrange("p (g t) -> p g t", g=4)
        ident = const(C_IDENT)

        def vec(name, n=None):
            at, size = VEC[name]
            return vecs[:, at:at + size] if n is None else vecs[:, at + n:at + n + 1]

        def region(kb, n):
            return arena[:, int(kb * 256):int(kb * 256) + n]

        def region3(kb, m, n):
            return region(kb, m * n).rearrange("p (m n) -> p m n", m=m)

        hT = region3(0, KD, S)
        wslot = [region3(16 + 16 * n, KD, HALF) for n in range(4)]
        fslot = [region(16 + 16 * n, 4 * D).rearrange("p (k n) -> p k n", k=4) for n in range(4)]
        qkvT = region3(80, QKV, S)
        zT = region3(104, H, S)
        xs_mix = region3(120, T, D)
        levelm = region3(48, LEVELS, P)
        duT = region(52, T * H * P).rearrange("p (c h n) -> p c h n", c=T, h=H)
        tmp = region3(60, 2, HALF)
        rows = region3(64, 4, D)
        poolx = region3(64, 4, 16 + S)
        poolpp = region3(72.5, 2, 16 + S)
        cacc = region3(144, 2, S)
        rn = region3(148, 2, S)
        sq = region3(152, 2, S)
        macc = region3(156, N_MODC, HALF)
        gacc = gtrow[:, :, :].rearrange("p k (b n) -> p (k b) n", b=2)
        mpair = gtrow[:, :, :].rearrange("p s (k n) -> p s k n", k=2)
        msingle = region3(168, 2, HALF)
        Am = region(120, T * H * P).rearrange("p (c h n) -> p c h n", c=T, h=H)
        Rm = region(128, T * H * P).rearrange("p (c h n) -> p c h n", c=T, h=H)
        Tm = region(136, T * H * P).rearrange("p (c h n) -> p c h n", c=T, h=H)
        egr = Tm
        kcdT = Tm
        uig = Rm
        Vm = region(0, T * H * P).rearrange("p (c h n) -> p c h n", c=T, h=H)
        Bm = region(8, T * H * P).rearrange("p (c h n) -> p c h n", c=T, h=H)
        kbe = region(144, T * H * P).rearrange("p (c h n) -> p c h n", c=T, h=H)
        kdec = region(152, T * H * P).rearrange("p (c h n) -> p c h n", c=T, h=H)
        vb = region(160, T * H * P).rearrange("p (c h n) -> p c h n", c=T, h=H)
        state = region(0, 2 * H * P).rearrange("p (b h n) -> p b h n", b=2, h=H)
        vnew = region(4, 2 * H * P).rearrange("p (b h n) -> p b h n", b=2, h=H)
        orms = region3(8, 4, S)
        ocat = region3(120, H, S)
        poolcat = region3(112, 4, S)
        wpool = region3(77, 4, P)

        def cat(k):
            return ocat[:, k, :] if k < H else poolcat[:, k - H, :]

        score = region(80, (T * PH + 1) * 2 * NK).rearrange("p (i s n) -> p i s n", s=2, n=NK)
        xn = region3(114, T, D)
        xcur = region(130, D)
        diag = region3(134, GRING, P)
        skT = region3(138, 2 * PH, P)
        qT = region3(146, 2, S)
        prow = region3(150, 2, D)
        junk = region(158, D)
        ring = [region(16 + 8 * n, 2 * D) for n in range(GRING)]
        def low3(kb, m, n):
            return r_low[:, int(kb * 256):int(kb * 256) + m * n].rearrange("p (m n) -> p m n", m=m)

        def high3(kb, m, n):
            return r_high[:, int((kb - 84) * 256):int((kb - 84) * 256) + m * n].rearrange("p (m n) -> p m n", m=m)

        def middle3(kb, m, n):
            return middle[:, int((kb - 48) * 256):int((kb - 48) * 256) + m * n].rearrange("p (m n) -> p m n", m=m)

        def upper3(kb, m, n):
            return upper[:, int((kb - 128) * 256):int((kb - 128) * 256) + m * n].rearrange("p (m n) -> p m n", m=m)

        a_hi, a_lo = low3(0, KD, S), low3(16, KD, S)
        u_hi = [low3(32 + 8 * n, KD, P) for n in range(2)]
        u_lo = [low3(36 + 8 * n, KD, P) for n in range(2)]
        raw = [middle3(48 + 16 * n, KD, HALF) for n in range(2)]
        rawrow = [middle3(48 + 16 * n, 4, D) for n in range(2)]

        def raw_unit(u):
            if u >= UNIT_FOUT:
                return rawrow[u // 4 % 2][:, u % 4, :].rearrange("p (m n) -> p m n", m=KD)
            w = raw[u // 4 % 2]
            if u >= UNIT_FIN:
                lo = (u % 2 * 2 + u % 4 // 2) * P
                return w[:, :, lo:lo + P]
            if u < 2 * KD:
                return w[:, :, u % 4 * P:(u % 4 + 1) * P]
            return w[:, u % 4 * 2:u % 4 * 2 + 2, :].rearrange("p k n -> p (k n)").rearrange("p (m n) -> p m n", m=KD)

        def halves(w):
            return w.rearrange("p m n -> p (m n)").rearrange("p (k n) -> p k n", k=2)

        qz = region3(80, AH, S)
        kT2 = region3(112, KD, S)
        v2 = upper3(128, T, D)
        xs2 = region3(144, T, D)
        y_hT = upper3(144, KD, S)
        ZW = 1280
        spb = [upper3(144 + 5 * n, 1, ZW)[:, 0, :] for n in range(3)]
        sp_hi, sp_lo = high3(159, 1, ZW)[:, 0, :], high3(164, 1, ZW)[:, 0, :]
        r_consts = high3(169, 4, P)
        R_IDENT, R_NEG, R_NLOW, R_NONE = range(4)
        act_hi, act_lo = high3(84, FT, S), high3(128, FT, S)
        ff = middle3(80, 2, S)
        tail = region3(0, 2, D)

        s = {}
        for name in ("x", "const", "vec", "wba", "level", "rows", "wpool", "skt", "prow", "out",
                     "own_act", "own_dve", "own_pool",
                     "ssq", "sd", "xs", "tr", "ht_act", "ht_dve",
                     "chunk_used", "proj", "ba", "conv", "silu", "pz", "poolx_free", "pooled", "poolmm", "poolcat",
                     "beta", "a2", "espn", "lnsp", "g", "gcum", "gsb", "egs", "uig", "grow", "growt", "growe",
                     "dexp", "masked", "sqr", "ss", "rsd", "rnorm", "kk", "ktok", "ktoks", "attn", "amat", "qd",
                     "bl", "r0", "inv0", "v", "vs", "rt", "upd", "kcd", "kcds", "vn", "vns", "sup", "state", "o", "os",
                     "macc", "gacc", "gates_out", "msum", "gsum", "mod", "osq", "oss", "ord", "onorm", "wout", "xa",
                     "q", "qs", "sc", "scs", "seln", "idx", "dots", "gate", "gates_e", "diag", "slot_done",
                     "acc", "acc_out", "zero", "fin", "qkv_a", "qkv_d", "z", "az", "lnp", "spd", "rest", "at", "av",
                     "y", "ysq", "yfree", "ffn", "ffs", "ffd", "cs", "pzero", "turn", "silz", "smx", "sexp",
                     "q_hi", "q_lo", "qh_hi", "qh_lo", "u_hi", "u_lo", "unit_used", "a_y", "a_hi", "a_lo", "rc", "sp_hi", "sp_lo", "o_hi", "o_lo"):
            s[name] = sem(name)
        w_early = [sem(f"w_early{n}") for n in range(2)]
        m_pair = [sem(f"m_pair{n}") for n in range(2)]
        m_single = [sem(f"m_single{n}") for n in range(2)]
        w_late = [sem(f"w_late{n}") for n in range(2)]
        gathered = [sem(f"gathered{n}") for n in range(GRING)]

        NORMS = 4
        block = ctx.enter_context(nc.Block())

        @block.sync
        def _(sp):
            sp.dma_start(vecs[:, :], a["vecs"]).then_inc(s["vec"], 16)
            sp.dma_start(x[:, :, :], a["x"].rearrange("(t p) d -> p t d", p=P)).then_inc(s["x"], 16)
            sp.dma_start(consts[:, :], a["consts"]).then_inc(s["const"], 16)
            sp.dma_start(wba[:, :, :], a["w_ba"]).then_inc(s["wba"], 16)

            def early(n):
                if n >= 2:
                    sp.wait_ge(s["chunk_used"], n - 1)
                sp.dma_start(wslot[n % 2], a["w_early"][n]).then_inc(w_early[n % 2], 16)

            def pair(u):
                if u >= 2:
                    sp.wait_ge(s["macc"], u - 1)
                sp.dma_start(mpair[:, u % 2], a["w_ada"][u // 4, :, u % 4 * 2:u % 4 * 2 + 2, :]).then_inc(m_pair[u % 2], 16)

            def single(u):
                if u >= 2:
                    sp.wait_ge(s["gacc"], u - 1)
                sp.dma_start(msingle[:, u % 2, :], a["w_ada"][N_MODC + u // KD, :, u % KD, :]).then_inc(m_single[u % 2], 16)

            early(0)
            early(1)
            sp.dma_start(wpool, a["w_pool"]).then_inc(s["wpool"], 16)
            sp.dma_start(levelm, a["levels"].rearrange("p (l n) -> p l n", l=LEVELS)).then_inc(s["level"], 16)
            for u in range(14):
                pair(u)
            early(2)
            for u in range(14, 26):
                pair(u)
            early(3)
            for u in range(26, 4 * N_MODC):
                pair(u)
            early(4)
            early(OUT0)
            sp.wait_ge(s["poolmm"], 4)
            sp.dma_start(rows, a["rows"].rearrange("r (o d) -> o r d", o=1).broadcast_to([P, 4, D])).then_inc(s["rows"], 16)
            early(OUT0 + 1)
            sp.wait_ge(s["msum"], 1)
            for u in range(KD * N_GATE):
                single(u)
            sp.wait_ge(s["os"], T)
            for n in range(N_QUERY):
                if n == 1:
                    sp.dma_start(prow, a["prow"].rearrange("r (o d) -> o r d", o=1).broadcast_to([P, 2, D])).then_inc(s["prow"], 16)
                    sp.dma_start(skT, a["sub_keys"]).then_inc(s["skt"], 16)
                    sp.wait_ge(s["gates_out"], N_GATE)
                if n >= 2:
                    sp.wait_ge(s["q_lo"], 4 * (n - 1))
                sp.dma_start(raw[n % 2], a["w_early"][QUERY0 + n]).then_inc(w_early[(QUERY0 + n) % 2], 16)
            sp.wait_ge(s["acc_out"], T)
            for m in range(LATE):
                if m >= 2:
                    sp.wait_ge(s["u_lo"], 4 * (m - 1))
                if m < FOUT0:
                    sp.dma_start(raw[m % 2], a["w_late"][m]).then_inc(w_late[m % 2], 16)
                else:
                    rows_of = min(4, FT - 4 * (m - FOUT0))
                    sp.dma_start(rawrow[m % 2][:, 0:rows_of, :], a["w_late"][m].rearrange("p k n -> p (k n)")[:, 0:rows_of * D].rearrange("p (k n) -> p k n", n=D)).then_inc(w_late[m % 2], 16)
            sp.wait_ge(s["fin"], T)
            sp.dma_start(out.rearrange("b (t p) d -> p (b t) d", p=P), x[:, :, :]).then_inc(s["out"], 16)
            sp.wait_ge(s["out"], 16)

        def act_stats(eng, own, k, ready, junk_of, first=None):
            for t in range(T):
                ready(t)
                if T * k + t > 0:
                    eng.wait_ge(s["ssq"], T * k + t)
                nc.scalar.activation(junk_of(t), x[:, t, :], ACT.Square,
                                     accum_out=stat[:, 0, t:t + 1]).then_inc(s["ssq"], 1)
            eng.wait_ge(s["ssq"], T * (k + 1))
            nc.scalar.activation(stat[:, 1, :], stat[:, 0, :], ACT.Sqrt, bias=EPS, scale=1.0 / D).then_inc(s["sd"], 1)

        def pe_transposes(eng, k, src):
            for t in range(T):
                eng.wait_ge(s["xs"], T * k + t + 1)
                for kd in range(KD):
                    ins = nc.tensor.transpose(ps[:, kd, t * P:(t + 1) * P], src[:, t, kd * P:(kd + 1) * P], ident)
                ins.then_inc(s["tr"], 1)

        def evac_hT(eng, k, which, scale=None, bias=None):
            eng.wait_ge(s["tr"], T * (k + 1))
            for kd in range(which, KD, 2):
                if which == 0:
                    nc.scalar.activation(hT[:, kd, :], ps[:, kd, :], ACT.Identity if bias else ACT.Copy,
                                         **({"bias": bias(kd)} if bias else {}),
                                         **({"scale": scale(kd)} if scale else {})).then_inc(s["ht_act"], 1)
                elif scale is None:
                    nc.vector.tensor_copy(hT[:, kd, :], ps[:, kd, :]).then_inc(s["ht_dve"], 1)
                elif bias is None:
                    nc.vector.tensor_scalar(hT[:, kd, :], ps[:, kd, :], scale(kd), None, ALU.mult).then_inc(s["ht_dve"], 1)
                else:
                    nc.vector.tensor_scalar(hT[:, kd, :], ps[:, kd, :], scale(kd), bias(kd), ALU.mult, ALU.add).then_inc(s["ht_dve"], 1)

        def wait_hT(eng, k):
            eng.wait_ge(s["ht_act"], KD // 2 * (k + 1))
            eng.wait_ge(s["ht_dve"], KD // 2 * (k + 1))

        def scale_of(name):
            return lambda kd: vec(name, kd)

        def stat_mod(k, kd):
            return modc[:, 2 * k + 1, kd:kd + 1]

        tail_sq = region(8, D)

        def out_pair(sc, i):
            sc.wait_ge(s["av"], 2 * i + 2)
            if i == 0:
                sc.wait_ge(s["unit_used"], UNIT_O2)
            nc.scalar.activation(a_hi[:, i, :], ps[:, 6 + i % 2, :], ACT.Copy).then_inc(s["o_hi"], 1)

        @block.tensor
        def _(pe):
            def mm(out_, lhsT, rhs, start=True, stop_=True, skip=False):
                return nc.tensor.matmul(out_, lhsT, rhs, start=start, stop=stop_, skip_group_check=skip)

            def landed(n):
                pe.wait_ge(w_early[n % 2], 16 * (n // 2 + 1))
                return wslot[n % 2]

            pe.wait_ge(s["const"], 16)
            pe_transposes(pe, 0, xs_mix)
            wait_hT(pe, 0)
            pe.wait_ge(s["wba"], 16)
            for t in range(T):
                for kd in range(KD):
                    ins = mm(ps[:, 0, t * 8:t * 8 + 8], hT[:, kd, t * P:(t + 1) * P], wba[:, kd, :], kd == 0, kd == KD - 1)
            ins.then_inc(s["ba"], 1)

            for j in range(20):
                w = landed(j // 4)
                if j >= 4:
                    if j - 4 < QKV:
                        pe.wait_ge(s["conv"], j - 3)
                    else:
                        pe.wait_ge(s["pz"], j - 4 - QKV + 1)
                for kd in range(KD):
                    ins = mm(ps[:, 1 + j % 4, :], w[:, kd, j % 4 * P:(j % 4 + 1) * P], hT[:, kd, :], kd == 0, kd == KD - 1)
                ins.then_inc(s["proj"], 1)
                if j % 4 == 3:
                    pe.wait_ge(s["proj"], j + 1)
                    nc.tensor.nop().then_inc(s["chunk_used"], 1)
                if j == 7:
                    pe.wait_ge(s["g"], 1)
                    mm(ps[:, 0, 32:48], const(C_UI), gates[:, 1, :])
                    mm(ps[:, 0, 48:64], const(C_ONES), gates[:, 1, :]).then_inc(s["gcum"], 1)
                if 8 <= j < 12:
                    c = j - 8
                    pe.wait_ge(s["uig"], c + 1)
                    if c >= 2:
                        pe.wait_ge(s["growt"], c - 1)
                        pe.wait_ge(s["growe"], c - 1)
                    mm(ps[:, 5 + c % 2, :], const(C_ONES), uig[:, c].rearrange("p h n -> p (h n)")).then_inc(s["grow"], 1)
                if j >= 12:
                    i = j - 12
                    pe.wait_ge(s["sqr"], i + 1)
                    if i == 0:
                        pe.wait_ge(s["growt"], T)
                        pe.wait_ge(s["growe"], T)
                    if i >= 2:
                        pe.wait_ge(s["rsd"], i - 1)
                    mm(ps[:, 5 + i % 2, :], const(C_ONES), sq[:, i % 2, :]).then_inc(s["ss"], 1)
            pe.wait_ge(s["macc"], 4 * N_MODC)
            for col in range(4 * KD):
                ins = mm(ps[:, 0, 64 + col:65 + col], macc[:, col // 4, col % 4 * P:(col % 4 + 1) * P], const(C_ONES)[:, 0:1])
            ins.then_inc(s["msum"], 1)
            pe.wait_ge(s["wpool"], 16)
            for g in range(4):
                pe.wait_ge(s["pooled"], g + 1)
                if g >= 1:
                    pe.wait_ge(s["poolcat"], g)
                mm(ps[:, 7, :], wpool[:, g, :], poolcat[:, g, :]).then_inc(s["poolmm"], 1)

            pe.wait_ge(s["rnorm"], 8)
            pe.wait_ge(s["pz"], 8)
            for n in range(2 * T):
                c, src = n % T, H + H * (n // T)
                if n >= T:
                    pe.wait_ge(s["ktoks"], 2 * (n - T + 1))
                if n == 0:
                    pe.wait_ge(s["poolcat"], 4)
                    pe.wait_ge(s["mod"], 1)
                for h in range(H):
                    ins = nc.tensor.transpose(ps[:, c, h * P:(h + 1) * P], qkvT[:, src + h, c * P:(c + 1) * P], ident)
                ins.then_inc(s["ktok"], 1)
            for c in range(T):
                if c == 0:
                    pe.wait_ge(s["rsd"], 8)
                for h in range(H):
                    ins = mm(ps[:, 4 + c, h * P:(h + 1) * P], qkvT[:, H + h, c * P:(c + 1) * P], qkvT[:, h, c * P:(c + 1) * P])
                ins.then_inc(s["attn"], 1)
            for c in range(T):
                pe.wait_ge(s["ktoks"], 2 * T + c + 1)
                for h in range(H):
                    ins = mm(ps[:, c, h * P:(h + 1) * P], qkvT[:, H + h, c * P:(c + 1) * P], qkvT[:, H + h, c * P:(c + 1) * P])
                ins.then_inc(s["kk"], 1)

            for c in range(T):
                pe.wait_ge(s["bl"], c + 1)
                pe.wait_ge(s["qd"], c + 1)
                for h in range(H):
                    ins = nc.tensor.transpose(ps[:, 4 + c, h * P:(h + 1) * P], Bm[:, c, h, :], ident)
                ins.then_inc(s["inv0"], 1)
            for lv in range(1, LEVELS):
                last = lv == LEVELS - 1
                for c in range(T):
                    pe.wait_ge(s["bl"], T * lv + c + 1)
                    pe.wait_ge(s["upd"], T * (lv - 1) + c + 1)
                    for h in range(H):
                        ins = mm(ps[:, c, h * P:(h + 1) * P], Bm[:, c, h, :], Rm[:, c, h, :])
                    ins.then_inc(s["v"], 1)
                for c in range(T):
                    pe.wait_ge(s["vs"], T * (lv - 1) + c + 1)
                    for h in range(H):
                        ins = mm(ps[:, c, h * P:(h + 1) * P], Tm[:, c, h, :], Vm[:, c, h, :])
                    if not last:
                        for h in range(H):
                            ins = mm(ps[:, 4 + c, h * P:(h + 1) * P], Vm[:, c, h, :], Tm[:, c, h, :])
                    ins.then_inc(s["rt"], 1)
            for c in range(T):
                pe.wait_ge(s["upd"], T * (LEVELS - 1) + c + 1)
                for h in range(H):
                    ins = mm(ps[:, c, h * P:(h + 1) * P], kbe[:, c, h, :], Rm[:, c, h, :])
                ins.then_inc(s["kcd"], 1)
            for c in range(T):
                for h in range(H):
                    if c > 0 and h == 0:
                        pe.wait_ge(s["state"], c)
                    if h == 0:
                        pe.wait_ge(s["kcds"], T)
                    ins = mm(ps[:, 4, h * P:(h + 1) * P], Rm[:, c, h, :], vb[:, c, h, :], True, c == 0)
                    if c > 0:
                        ins = mm(ps[:, 4, h * P:(h + 1) * P], kcdT[:, c, h, :], state[:, (c - 1) % 2, h, :], False, True)
                ins.then_inc(s["vn"], 1)
                pe.wait_ge(s["vns"], c + 1)
                if c < T - 1:
                    for h in range(H):
                        ins = mm(ps[:, 5, h * P:(h + 1) * P], kdec[:, c, h, :], vnew[:, c % 2, h, :])
                    ins.then_inc(s["sup"], 1)
                if c >= 1:
                    pe.wait_ge(s["os"], c)
                for h in range(H):
                    if c > 0:
                        mm(ps[:, 6, h * P:(h + 1) * P], state[:, (c - 1) % 2, h, :], qkvT[:, h, c * P:(c + 1) * P], True, False)
                    ins = mm(ps[:, 6, h * P:(h + 1) * P], vnew[:, c % 2, h, :], duT[:, c, h, :], c == 0, True)
                ins.then_inc(s["o"], 1)
            for h in range(H):
                pe.wait_ge(s["osq"], h + 1)
                mm(ps[:, 4 + h, :], const(C_ONES), orms[:, h, :]).then_inc(s["oss"], 1)
            for n in range(N_OUT):
                w = landed(OUT0 + n)
                for kds in (range(H, KD), range(H)):
                    if n == 0 and kds.start == 0:
                        pe.wait_ge(s["onorm"], H)
                    for t in range(T):
                        for kd in kds:
                            ins = mm(ps[:, n * 4 + t, :], cat(kd)[:, t * P:(t + 1) * P], w[:, kd, :], kd == H, kd == H - 1)
                        if kds.start == 0:
                            ins.then_inc(s["wout"], 1)
                pe.wait_ge(s["wout"], 4 * n + 4)
                nc.tensor.nop().then_inc(s["chunk_used"], 1)

            pe.wait_ge(s["xa"], 2 * T)
            pe_transposes(pe, 1, xn)
            pe.wait_ge(s["gacc"], KD * N_GATE)
            pe.wait_ge(s["qh_lo"], KD)
            for m in range(N_GATE):
                mm(ps[:, 4 + m, :], const(C_ONES), gacc[:, m, :]).then_inc(s["gsum"], 1)
            pe.wait_ge(s["skt"], 16)
            for j in range(2 * PH + 1):
                if j < 2 * PH:
                    pe.wait_ge(s["q_lo"], j + 1)
                    if j >= 2:
                        pe.wait_ge(s["qs"], j - 1)
                    bank = ps[:, j % 2, :]
                    for kd in range(KD):
                        mm(bank, u_hi[j % 2][:, kd, :], a_hi[:, kd, :], kd == 0, False)
                        mm(bank, u_hi[j % 2][:, kd, :], a_lo[:, kd, :], False, False)
                        ins = mm(bank, u_lo[j % 2][:, kd, :], a_hi[:, kd, :], False, kd == KD - 1)
                    ins.then_inc(s["q"], 1)
                if j >= 1:
                    i = j - 1
                    pe.wait_ge(s["qs"], i + 1)
                    if i >= 2:
                        pe.wait_ge(s["scs"], i - 1)
                    for t in range(T):
                        ins = mm(ps[:, 2 + i % 2, t * P:(t + 1) * P], qT[:, i % 2, t * P:(t + 1) * P], skT[:, i, :])
                    ins.then_inc(s["sc"], 1)

            pe.wait_ge(s["gates_out"], N_GATE)
            nc.tensor.nop().then_inc(s["slot_done"], GRING)
            pe.wait_ge(s["scs"], 2 * PH)
            with pe.Fori(0, T) as t:
                for n in range(2):
                    mm(ps[:, 4 + n, :], ident, x[:, bass.ds(t, 1), n * HALF:(n + 1) * HALF].rearrange("p a n -> p (a n)"), True, False, True)
                with pe.Fori(0, PH // 2) as hp:
                    for k in range(2 * TOPK):
                        if k % BATCH == 0:
                            pe.wait_ge(s["diag"], (t * (PH // 2) + hp) * (2 * TOPK) + (k + BATCH))
                        for n in range(2):
                            ins = mm(ps[:, 4 + n, :], diag[:, k % GRING, :], ring[k % GRING][:, D + n * HALF:D + (n + 1) * HALF], False, False, True)
                        ins.then_inc(s["slot_done"], 1)
                pe.wait_ge(s["slot_done"], (t + 1) * (PH * TOPK) + GRING)
                nc.tensor.nop().then_inc(s["acc"], 1)
                pe.wait_ge(s["acc_out"], t + 1)

            def split_tile(out_, u, k, rows_hi, rows_lo):
                for kd in range(KD):
                    if u in (0, UNIT_FIN):
                        pe.wait_ge(s["a_lo"], KD * k + kd + 1)
                    mm(out_, u_hi[u % 2][:, kd, :], rows_hi[:, kd, :], kd == 0, False)
                    mm(out_, u_hi[u % 2][:, kd, :], rows_lo[:, kd, :], False, False)
                    ins = mm(out_, u_lo[u % 2][:, kd, :], rows_hi[:, kd, :], False, kd == KD - 1)
                return ins.then_inc(s["unit_used"], 1)

            def split_rows(out_of, u, k_of, cols_hi, cols_lo, kts, first, last):
                w_hi, w_lo = halves(u_hi[u % 2]), halves(u_lo[u % 2])
                for t in range(T):
                    tok = slice(t * P, (t + 1) * P)
                    for hf in range(2):
                        kt, n = k_of(hf)
                        begin, end = kt == first, kt == last
                        mm(out_of(t, n), cols_hi[:, kt, tok], w_hi[:, hf, :], begin, False)
                        mm(out_of(t, n), cols_hi[:, kt, tok], w_lo[:, hf, :], False, False)
                        ins = mm(out_of(t, n), cols_lo[:, kt, tok], w_hi[:, hf, :], False, end)
                    if t < T - 1 and end and kts is not None:
                        ins.then_inc(s[kts], 1)
                return ins.then_inc(s["unit_used"], 1)

            def unit(u):
                pe.wait_ge(s["u_lo"], u + 1)

            pe_transposes(pe, 2, xs2)
            for m in range(24):
                unit(m)
                if m < 16:
                    if m >= 8:
                        pe.wait_ge(s["qkv_a" if m % 2 == 0 else "qkv_d"], (m - 8) // 2 + 1)
                    split_tile(ps[:, m % 8, :], m, 0, a_hi, a_lo)
                else:
                    if m % 4 == 0:
                        pe.wait_ge(s["qkv_a"], (m - 8 + 4) // 2)
                        pe.wait_ge(s["qkv_d"], (m - 8 + 4) // 2)
                    split_rows(lambda t, n: ps[:, m // 4 % 2 * 4 + t, :], m, lambda hf: (m % 4 * 2 + hf, 0),
                               a_hi, a_lo, None, 0, KD - 1)
            pe.wait_ge(s["qkv_a"], 12)
            pe.wait_ge(s["qkv_d"], 12)
            ZAT = [0, 512, 1024, 896]

            def zcols(h, sb_, lo=0):
                base = (h % 2) * 1536 + ZAT[sb_] + lo
                return psf[:, base:(h % 2) * 1536 + ZAT[sb_] + S - sb_ * P]

            for step in range(AH + 2):
                h = step
                if h < AH:
                    if h >= 2:
                        pe.wait_ge(s["at"], h - 1)
                    for b in range(T):
                        mm(zcols(h, b), kT2[:, h // 2, b * P:(b + 1) * P], qz[:, h, b * P:S], b != 3, False, True)
                        if h == 0 and b == 0:
                            pe.wait_ge(s["rc"], 4)
                        ins = mm(zcols(h, b)[:, 0:P], r_consts[:, R_IDENT, :], r_consts[:, R_NEG, :], False, False, True)
                    ins.then_inc(s["z"], 1)
                h = step - 2
                if h >= 0:
                    pe.wait_ge(s["at"], h + 1)
                    if h % 2 == 0 and h >= 4:
                        pe.wait_ge(s["o_lo"], h // 2 - 1)
                    lo = h % 2 * 64
                    for b in range(T):
                        ins = mm(ps[lo:lo + 64, 6 + h // 2 % 2, b * P:S], v2[:, b, h * 64:(h + 1) * 64],
                                 spb[h % 3][:, ZAT[b]:ZAT[b] + S - b * P], b == 0, b == T - 1, True)
                    ins.then_inc(s["av"], 1)
                h = step - 1
                if 0 <= h < AH:
                    pe.wait_ge(s["sp_lo"], h + 1)
                    for b in range(T):
                        for b2 in range(b, T):
                            for part in (sp_hi, sp_lo):
                                ins = mm(zcols(h, b, (b2 - b) * P), r_consts[:, R_NLOW if b2 == b else R_NONE, :],
                                         part[:, ZAT[b2]:ZAT[b2] + S - b2 * P], False, b2 == T - 1 and part is sp_lo, True)
                    ins.then_inc(s["rest"], 1)
            pe.wait_ge(s["o_lo"], AH // 2)
            for m in range(4 * N_O2):
                unit(UNIT_O2 + m)
                split_rows(lambda t, n: ps[:, 2 * t + n, :], UNIT_O2 + m, lambda hf: (m % 4 * 2 + hf, m // 4),
                           a_hi, a_lo, "y" if m // 4 == 1 else None, 0, KD - 1)
            pe.wait_ge(s["unit_used"], UNIT_FIN)
            nc.tensor.nop().then_inc(s["y"], 1)
            pe.wait_ge(s["yfree"], T)
            pe_transposes(pe, 3, xs2)
            for j in range(FT):
                if j >= 4:
                    pe.wait_ge(s["ffd"], j - 3)
                for n in range(2):
                    unit(UNIT_FIN + 2 * j + n)
                    split_tile(ps[:, 2 * j % 8 + n, :], UNIT_FIN + 2 * j + n, 1, a_hi, a_lo)
            pe.wait_ge(s["ffd"], FT)
            for kt in range(FT):
                unit(UNIT_FOUT + kt)
                split_rows(lambda t, n: ps[:, 2 * t + n, :], UNIT_FOUT + kt, lambda hf: (kt, hf),
                           act_hi, act_lo, "y", 0, FT - 1)
            pe.wait_ge(s["unit_used"], UNITS)
            nc.tensor.nop().then_inc(s["y"], 1)

        @block.scalar
        def _(sc):
            own = Own(sc, s["own_act"])
            sc.wait_ge(s["vec"], 16)
            nc.scalar.activation(ccol[:, :], vec("c"), ACT.Silu).then_inc(s["cs"], 1)
            sc.wait_ge(s["x"], 16)
            act_stats(sc, own, 0, lambda t: None, lambda t: xs_mix[:, t, :])
            evac_hT(sc, 0, 0, scale_of("norm_mix"))
            sc.wait_ge(s["ba"], 1)
            ba = ps[:, 0, 0:32].rearrange("p (t k) -> p t k", k=8)
            beta = gates[:, 0, :].rearrange("p (t h) -> p t h", h=H)
            sc.wait_ge(s["a2"], 1)
            nc.scalar.activation(beta, ba[:, :, 0:H], ACT.Sigmoid).then_inc(s["beta"], 1)
            nc.scalar.preload_act_table_set("natural_log_exp_and_others")
            own.step(nc.scalar.activation(gates[:, 3, :], gates[:, 3, :], ACT.Exp))
            nc.scalar.activation(ealog[:, :], vec("alog"), ACT.Exp)
            nc.scalar.activation(gates[:, 3, :], gates[:, 3, :], ACT.Ln, bias=1.0).then_inc(s["lnsp"], 1)

            def silu(j):
                sc.wait_ge(s["conv"], j + 1)
                nc.scalar.activation(qkvT[:, j, :], cacc[:, j % 2, :], ACT.Silu).then_inc(s["silu"], 1)

            for j in range(8):
                silu(j)
            sc.wait_ge(s["gsb"], 1)
            nc.scalar.activation(gates[:, 6, :], gates[:, 4, :], ACT.Exp)
            nc.scalar.activation(gates[:, 7, :], gates[:, 5, :], ACT.Exp)
            nc.scalar.activation(gates[:, 8, :], gates[:, 9, :], ACT.Exp).then_inc(s["egs"], 1)

            def decays(c):
                sc.wait_ge(s["growt"], c + 1)
                nc.scalar.activation(egr[:, c].rearrange("p h n -> p (h n)"), ps[:, 5 + c % 2, :], ACT.Exp).then_inc(s["growe"], 1)
                nc.scalar.activation(duT[:, c].rearrange("p h n -> p (h n)"), tmp[:, 0, :], ACT.Exp).then_inc(s["dexp"], 1)
                nc.scalar.activation(Am[:, c].rearrange("p h n -> p (h n)"), tmp[:, 1, :], ACT.Exp, scale=-1.0).then_inc(s["dexp"], 1)

            for c in range(T):
                decays(c)
            for j in range(8, QKV):
                silu(j)

            def square(i):
                if i >= 2:
                    sc.wait_ge(s["ss"], i - 1)
                nc.scalar.activation(sq[:, i % 2, :], qkvT[:, i, :], ACT.Square).then_inc(s["sqr"], 1)

            sc.wait_ge(s["silu"], QKV)
            square(0)
            for i in range(8):
                sc.wait_ge(s["proj"], 13 + i)
                dst = poolx[:, i, 16:16 + S] if i < 4 else zT[:, i - 4, :]
                nc.scalar.activation(dst, ps[:, 1 + i % 4, :], ACT.Copy).then_inc(s["pz"], 1)
                if i + 1 < 8:
                    square(i + 1)
                sc.wait_ge(s["ss"], i + 1)
                if i >= 2:
                    sc.wait_ge(s["rnorm"], i - 1)
                nc.scalar.activation(rn[:, i % 2, :], ps[:, 5 + i % 2, :], ACT.Sqrt, bias=EPS).then_inc(s["rsd"], 1)
            for g in range(4):
                sc.wait_ge(s["poolmm"], g + 1)
                nc.scalar.activation(poolcat[:, g, :], ps[:, 7, :], ACT.Copy, scale=vec("pool", g)).then_inc(s["poolcat"], 1)
            sc.wait_ge(s["pz"], 8)
            nc.scalar.activation(zT, zT, ACT.Silu).then_inc(s["silz"], 1)
            for lv in range(1, LEVELS):
                for c in range(T):
                    sc.wait_ge(s["v"], T * (lv - 1) + c + 1)
                    nc.scalar.activation(Vm[:, c].rearrange("p h n -> p (h n)"), ps[:, c, :], ACT.Copy).then_inc(s["vs"], 1)
            for c in range(T):
                sc.wait_ge(s["kcd"], c + 1)
                nc.scalar.activation(kcdT[:, c].rearrange("p h n -> p (h n)"), ps[:, c, :], ACT.Copy, scale=-1.0).then_inc(s["kcds"], 1)
            for c in range(T):
                sc.wait_ge(s["vn"], c + 1)
                nc.scalar.activation(vnew[:, c % 2].rearrange("p h n -> p (h n)"), ps[:, 4, :], ACT.Copy).then_inc(s["vns"], 1)
                sc.wait_ge(s["o"], c + 1)
                nc.scalar.activation(ocat[:, :, c * P:(c + 1) * P], ps[:, 6, :].rearrange("p (h n) -> p h n", h=H), ACT.Copy).then_inc(s["os"], 1)
            sc.wait_ge(s["os"], T)
            for h in range(H):
                nc.scalar.activation(orms[:, h, :], ocat[:, h, :], ACT.Square).then_inc(s["osq"], 1)
            for h in range(H):
                sc.wait_ge(s["oss"], h + 1)
                nc.scalar.activation(orms[:, h, :], ps[:, 4 + h, :], ACT.Sqrt, bias=EPS, scale=1.0 / P).then_inc(s["ord"], 1)
            act_stats(sc, own, 1, lambda t: sc.wait_ge(s["xa"], T + t + 1), lambda t: junk)

            def split_query(j):
                if j >= 2 * PH:
                    return
                if j % 4 == 0:
                    n = QUERY0 + j // 4
                    sc.wait_ge(w_early[n % 2], 16 * (n // 2 + 1))
                if j >= 2:
                    sc.wait_ge(s["q"], j - 1)
                nc.scalar.activation(u_hi[j % 2], raw_unit(j), ACT.Copy).then_inc(s["q_hi"], 1)

            split_query(0)
            split_query(1)
            sc.wait_ge(s["tr"], 2 * T)
            for kd in range(KD):
                nc.scalar.activation(a_hi[:, kd, :], ps[:, kd, :], ACT.Copy).then_inc(s["qh_hi"], 1)
            for j in range(2 * PH):
                sc.wait_ge(s["q"], j + 1)
                if j >= 2:
                    sc.wait_ge(s["sc"], j - 1)
                nc.scalar.activation(qT[:, j % 2, :], ps[:, j % 2, :], ACT.Copy).then_inc(s["qs"], 1)
                split_query(j + 2)
            dots = sel[:, 1000:1008]
            gel = sel[:, 1008:1016]
            wgt = sel[:, 1016:1024]
            sexp = lambda par: sel[:, 1024 + 16 * par:1040 + 16 * par]
            ssum = lambda par: sel[:, 1056 + par:1057 + par]
            gate = lambda par: sel[:, 1060 + 16 * par:1076 + 16 * par]
            nmax = lambda par: sel[:, 1100 + par:1101 + par]
            tops = lambda par: sel[:, 1104 + 16 * par:1120 + 16 * par]

            def soft(n, par):
                sc.wait_ge(s["smx"], n)
                nc.scalar.activation(sexp(par), tops(par), ACT.Exp, bias=nmax(par), accum_out=ssum(par)).then_inc(s["sexp"], 1)

            soft(1, 0)
            with sc.Fori(0, T) as t:
                with sc.Fori(0, PH // 2) as hp:
                    it = t * (PH // 2) + hp
                    for b in range(2 * TOPK // BATCH):
                        k0 = b * BATCH
                        p2 = b % 2
                        col = slice(4 * p2, 4 * p2 + 4)
                        par = b // 4
                        sc.wait_ge(s["dots"], it * 8 + (b + 1))
                        nc.scalar.activation(gel[:, col], dots[:, col], ACT.Gelu).then_inc(s["own_act"], 1)
                        sc.wait_ge(s["own_act"], it * 40 + (b * 5 + 2))
                        if b % 4 == 0:
                            sc.wait_ge(s["gate"], it * 2 + (par + 1))
                        for k in range(BATCH):
                            nc.scalar.activation(wgt[:, 4 * p2 + k:4 * p2 + k + 1], gel[:, 4 * p2 + k:4 * p2 + k + 1], ACT.Copy,
                                                 scale=gate(par)[:, k0 % TOPK + k:k0 % TOPK + k + 1]).then_inc(s["own_act"], 1)
                        sc.wait_ge(s["slot_done"], it * 32 + (k0 + 4))
                        sc.wait_ge(s["own_act"], it * 40 + (b * 5 + 6))
                        for k in range(BATCH):
                            nc.scalar.activation(diag[:, (k0 + k) % GRING, :], ident, ACT.Copy,
                                                 scale=wgt[:, 4 * p2 + k:4 * p2 + k + 1]).then_inc(s["diag"], 1)
                        if b % 4 == 2:
                            soft(it * 2 + (par + 2), 1 - par)
                sc.wait_ge(s["acc"], t + 1)
                nc.scalar.activation(x[:, bass.ds(t, 1), :], ps[:, 4:6, :].rearrange("p b n -> p (b n)").rearrange("p (o n) -> p o n", o=1), ACT.Copy).then_inc(s["acc_out"], 1)
            sc.wait_ge(s["acc_out"], T)
            act_stats(sc, own, 2, lambda t: None, lambda t: junk)
            act_stats(sc, own, 3, lambda t: sc.wait_ge(s["seln"], t + 1), lambda t: junk)

            def split(u):
                if u >= UNITS:
                    return
                if u % 4 == 0:
                    sc.wait_ge(w_late[u // 4 % 2], 16 * (u // 8 + 1))
                if u >= 2:
                    sc.wait_ge(s["unit_used"], u - 1)
                else:
                    sc.wait_ge(s["acc"], T)
                nc.scalar.activation(u_hi[u % 2], raw_unit(u), ACT.Copy).then_inc(s["u_hi"], 1)

            def evac_y(k):
                sc.wait_ge(s["tr"], T * (k + 3))
                for kd in range(KD):
                    nc.scalar.activation(y_hT[:, kd, :], ps[:, kd, :], ACT.Identity, bias=modc[:, 2 * k, kd:kd + 1],
                                         scale=stat_mod(k, kd)).then_inc(s["a_y"], 1)

            split(0)
            split(1)
            evac_y(0)
            for i, c in enumerate((C_IDENT, C_NEG, C_NLOW, C_NONE)):
                nc.scalar.activation(r_consts[:, i, :], const(c), ACT.Copy).then_inc(s["rc"], 1)
            for m in range(0, 24):
                if m % 2 == 0:
                    sc.wait_ge(s["unit_used"], m + 1 if m < 16 else m // 4 * 4 + 4)
                    if m < 8:
                        if m == 0:
                            sc.wait_ge(s["zero"], 2)
                        nc.scalar.activation(qz[0:64, 2 * m, :], ps[0:64, m % 8, :], ACT.Copy, scale=0.125)
                        nc.scalar.activation(qz[64:128, 2 * m + 1, :], ps[64:128, m % 8, :], ACT.Copy, scale=0.125).then_inc(s["qkv_a"], 1)
                    elif m < 16:
                        nc.scalar.activation(kT2[:, m - 8, :], ps[:, m % 8, :], ACT.Copy).then_inc(s["qkv_a"], 1)
                    else:
                        nc.scalar.activation(v2[:, m % 4, (m - 16) // 4 * HALF:((m - 16) // 4 + 1) * HALF], ps[:, m % 8, :], ACT.Copy).then_inc(s["qkv_a"], 1)
                if m < 16:
                    split(m + 2)
                    if m == 15:
                        split(18)
                        split(19)
                        split(20)
                        split(21)
                elif m == 18:
                    for u in range(22, 26):
                        split(u)
            nc.scalar.preload_act_table_set("natural_log_exp_and_others")
            for step in range(AH + 1):
                h = step
                if h < AH:
                    sc.wait_ge(s["z"], h + 1)
                    if h == 0:
                        sc.wait_ge(s["a_lo"], KD)
                    if h >= 3:
                        sc.wait_ge(s["av"], h - 2)
                    zz = psf[:, h % 2 * 1536:h % 2 * 1536 + ZW]
                    nc.scalar.activation(spb[h % 3], zz, ACT.Abs).then_inc(s["lnp"], 1)
                    sc.wait_ge(s["lnp"], 3 * h + 1)
                    nc.scalar.activation(spb[h % 3], spb[h % 3], ACT.Exp, scale=-1.0).then_inc(s["lnp"], 1)
                    sc.wait_ge(s["lnp"], 3 * h + 2)
                    nc.scalar.activation(spb[h % 3], spb[h % 3], ACT.Ln, bias=1.0).then_inc(s["lnp"], 1)
                h = step - 1
                if h >= 0:
                    sc.wait_ge(s["rest"], h + 1)
                    nc.scalar.activation(spb[h % 3], psf[:, h % 2 * 1536:h % 2 * 1536 + ZW], ACT.Exp).then_inc(s["at"], 1)
                    if h % 2 == 0 and h >= 2:
                        out_pair(sc, h // 2 - 1)
            out_pair(sc, AH // 2 - 1)
            for u in range(UNIT_O2 + 2, UNIT_FIN + 2):
                split(u)

            def branch(k):
                for t in range(T):
                    sc.wait_ge(s["y"], T * k + t + 1)
                    if k + t > 0:
                        sc.wait_ge(s["ysq"], (T + 1) * k + t)
                    nc.scalar.activation(tail_sq, ps[:, 2 * t:2 * t + 2, :].rearrange("p b n -> p (b n)"), ACT.Square,
                                         accum_out=stat[:, 2, t:t + 1]).then_inc(s["ysq"], 1)
                sc.wait_ge(s["ysq"], (T + 1) * k + T)
                nc.scalar.activation(stat[:, 3, :], stat[:, 2, :], ACT.Sqrt, bias=EPS, scale=1.0 / D).then_inc(s["ysq"], 1)

            branch(0)
            act_stats(sc, own, 4, lambda t: sc.wait_ge(s["yfree"], t + 1), lambda t: tail_sq)
            evac_y(1)
            for j in range(FT):
                split(UNIT_FIN + 2 * j + 2)
                sc.wait_ge(s["unit_used"], UNIT_FIN + 2 * j + 2)
                if j >= 2:
                    sc.wait_ge(s["ffd"], j - 1)
                nc.scalar.activation(ff[:, j % 2, :], ps[:, 2 * j % 8, :], ACT.Silu).then_inc(s["ffs"], 1)
                split(UNIT_FIN + 2 * j + 3)
            for u in range(UNIT_FOUT + 2, UNITS):
                split(u)
            branch(1)

        @block.gpsimd
        def _(pl):
            pl.wait_ge(s["x"], 16)
            nc.gpsimd.memset(poolx[:, :, 0:16], 0.0).then_inc(s["pzero"], 1)
            nc.gpsimd.memset(poolpp[:, :, 0:16], 0.0).then_inc(s["pzero"], 1)

            own_pool = Own(pl, s["own_pool"])

            def modulation(chunks):
                for u in range(4 * chunks.start, 4 * chunks.stop):
                    n, kd = u // 4, u % 4 * 2
                    w = mpair[:, u % 2]
                    pl.wait_ge(m_pair[u % 2], 16 * (u // 2 + 1))
                    c = ccol[:, kd:kd + 2].rearrange("p (k o) -> p k o", o=1).broadcast_to([P, 2, HALF])
                    own_pool.step(nc.gpsimd.tensor_tensor(w, w, c, ALU.mult))
                    if kd == 0:
                        ins = nc.gpsimd.tensor_tensor(macc[:, n, :], w[:, 0, :], w[:, 1, :], ALU.add)
                    else:
                        own_pool.step(nc.gpsimd.tensor_tensor(w[:, 0, :], w[:, 0, :], w[:, 1, :], ALU.add))
                        pl.wait_ge(s["macc"], u)
                        ins = nc.gpsimd.tensor_tensor(macc[:, n, :], macc[:, n, :], w[:, 0, :], ALU.add)
                    ins.then_inc(s["macc"], 1)

            pl.wait_ge(s["cs"], 1)
            modulation(range(0, 3))
            pl.wait_ge(s["const"], 16)
            pl.wait_ge(s["g"], 1)
            ui4 = const(C_UI).rearrange("p (o n) -> p o n", o=1).broadcast_to([P, H, P])
            ls4 = const(C_LS).rearrange("p (o n) -> p o n", o=1).broadcast_to([P, H, P])

            def gcol(row, c):
                return gates[:, row, c * H:(c + 1) * H].rearrange("p (h o) -> p h o", o=1).broadcast_to([P, H, P])

            for c in range(T):
                if c == 0:
                    pl.wait_ge(s["xs"], T)
                    pl.wait_ge(s["tr"], T)
                nc.gpsimd.tensor_tensor(uig[:, c], ui4, gcol(1, c), ALU.mult).then_inc(s["uig"], 1)
            modulation(range(3, 6))
            pl.wait_ge(s["beta"], 1)
            for c in range(T):
                pl.wait_ge(s["dexp"], 2 * c + 2)
                nc.gpsimd.tensor_tensor(duT[:, c], duT[:, c], ui4, ALU.mult).then_inc(s["masked"], 1)
                own_pool.step(nc.gpsimd.tensor_tensor(Am[:, c], Am[:, c], ls4, ALU.mult))
                nc.gpsimd.tensor_tensor(Am[:, c], Am[:, c], gcol(0, c), ALU.mult).then_inc(s["masked"], 1)
            modulation(range(6, N_MODC))
            pl.wait_ge(s["level"], 16)
            for lv in range(LEVELS):
                m4 = levelm[:, lv, :].rearrange("p (o n) -> p o n", o=1).broadcast_to([P, H, P])
                for c in range(T):
                    if lv == 0:
                        pl.wait_ge(s["amat"], c + 1)
                        if c == 0:
                            pl.wait_ge(s["proj"], 20)
                    elif lv == 1:
                        pl.wait_ge(s["inv0"], c + 1)
                        pl.wait_ge(s["upd"], c + 1)
                    else:
                        pl.wait_ge(s["v"], T * (lv - 2) + c + 1)
                    nc.gpsimd.tensor_tensor(Bm[:, c], Am[:, c], m4, ALU.mult).then_inc(s["bl"], 1)
            pl.wait_ge(s["macc"], 4 * N_MODC)
            for u in range(KD * N_GATE):
                kd, acc, w = u % KD, gacc[:, u // KD, :], msingle[:, u % 2, :]
                pl.wait_ge(m_single[u % 2], 16 * (u // 2 + 1))
                c = ccol[:, kd:kd + 1].broadcast_to([P, HALF])
                if kd == 0:
                    ins = nc.gpsimd.tensor_tensor(acc, w, c, ALU.mult)
                else:
                    own_pool.step(nc.gpsimd.tensor_tensor(w, w, c, ALU.mult))
                    pl.wait_ge(s["gacc"], u)
                    ins = nc.gpsimd.tensor_tensor(acc, acc, w, ALU.add)
                ins.then_inc(s["gacc"], 1)
            for j in range(2 * PH):
                pl.wait_ge(s["q_hi"], j + 1)
                nc.gpsimd.tensor_tensor(u_lo[j % 2], raw_unit(j), u_hi[j % 2], ALU.subtract).then_inc(s["q_lo"], 1)
            heads, slots = pl.alloc_register("heads"), pl.alloc_register("slots")
            pl.reg_mov(heads, 0)
            pl.reg_mov(slots, 0)
            with pl.Fori(0, T * PH // 2):
                for k in range(2 * TOPK):
                    par = k // TOPK
                    pl.reg_add(slots, slots, 1)
                    if k % TOPK == 0:
                        pl.reg_add(heads, heads, 1)
                    pl.wait_ge(s["const"], 16)
                    pl.wait_ge(s["slot_done"], slots)
                    if k % TOPK == 0:
                        pl.wait_ge(s["idx"], heads)
                    nc.gpsimd.indirect_dma_start(
                        ring[k % GRING], None, a["experts"],
                        bass.IndirectOffsetOnAxis(ap=selu[:, par * 16 + k % TOPK:par * 16 + k % TOPK + 1], axis=0),
                    ).then_inc(gathered[k % GRING], 16)
            for u in range(UNITS):
                pl.wait_ge(s["u_hi"], u + 1)
                if u == 2:
                    pl.wait_ge(s["zero"], 2)
                nc.gpsimd.tensor_tensor(u_lo[u % 2], raw_unit(u), u_hi[u % 2], ALU.subtract).then_inc(s["u_lo"], 1)
                if u == 1:
                    pl.wait_ge(s["acc_out"], T)
                    pl.wait_ge(s["u_lo"], 2)
                    nc.gpsimd.memset(qz[64:128, 0:AH:2, :], 0.0).then_inc(s["zero"], 1)
                    nc.gpsimd.memset(qz[0:64, 1:AH:2, :], 0.0).then_inc(s["zero"], 1)

        @block.vector
        def _(ve):
            own = Own(ve, s["own_dve"])
            tt, ts, stt = nc.vector.tensor_tensor, nc.vector.tensor_scalar, nc.vector.scalar_tensor_tensor

            def rstd(k):
                ve.wait_ge(s["sd"], k + 1)
                own.step(nc.vector.reciprocal(stat[:, 1, :], stat[:, 1, :]))

            ve.wait_ge(s["x"], 16)
            rstd(0)
            for t in range(T):
                ts(xs_mix[:, t, :], x[:, t, :], stat[:, 1, t:t + 1], None, ALU.mult).then_inc(s["xs"], 1)
            ve.wait_ge(s["vec"], 16)
            evac_hT(ve, 0, 1, scale_of("norm_mix"))
            ve.wait_ge(s["ba"], 1)
            ba = ps[:, 0, 0:32].rearrange("p (t k) -> p t k", k=8)

            def th(n):
                return gates[:, n, :].rearrange("p (t h) -> p t h", h=H)

            def bch(ap):
                return ap.rearrange("p (o h) -> p o h", o=1).broadcast_to([P, T, H])

            own.step(tt(th(2), ba[:, :, H:2 * H], bch(vec("dtb")), ALU.add))
            stt(gates[:, 3, :], gates[:, 2, :], -1.0, gates[:, 2, :], ALU.mult, ALU.min).then_inc(s["a2"], 1)
            ve.wait_ge(s["lnsp"], 1)
            own.step(stt(gates[:, 2, :], gates[:, 2, :], 0.0, gates[:, 3, :], ALU.max, ALU.add))
            stt(th(1), th(2), -1.0, bch(ealog[:, :]), ALU.mult, ALU.mult).then_inc(s["g"], 1)

            def conv(j):
                ve.wait_ge(s["proj"], j + 1)
                if j >= 2:
                    ve.wait_ge(s["silu"], j - 1)
                px, acc = ps[:, 1 + j % 4, :], cacc[:, j % 2, :]
                w = lambda tap: vec("conv", CW * j + tap)
                own.step(ts(acc, px, w(CW - 1), None, ALU.mult))
                for sh in range(1, CW):
                    ins = stt(acc[:, sh:S], px[:, 0:S - sh], w(CW - 1 - sh), acc[:, sh:S], ALU.mult, ALU.add)
                    if sh < CW - 1:
                        own.step(ins)
                    else:
                        ins.then_inc(s["conv"], 1)

            for j in range(8):
                conv(j)
            ve.wait_ge(s["gcum"], 1)
            own.step(nc.vector.tensor_copy(gates[:, 4:6, :], ps[:, 0, 32:64].rearrange("p (a n) -> p a n", a=2)))
            tt(gates[:, 9, :], gates[:, 5, :], gates[:, 4, :], ALU.subtract).then_inc(s["gsb"], 1)
            ve.wait_ge(s["egs"], 1)
            ve.wait_ge(s["beta"], 1)
            own.step(tt(gates[:, 10, :], gates[:, 0, :], gates[:, 6, :], ALU.mult))

            def gcol(row, c):
                return gates[:, row, c * H:(c + 1) * H].rearrange("p (h o) -> p h o", o=1).broadcast_to([P, H, P])

            def v4(ap):
                return ap.rearrange("p (h n) -> p h n", h=H)

            def growth(c):
                ve.wait_ge(s["grow"], c + 1)
                if c >= 1:
                    ve.wait_ge(s["dexp"], 2 * c)
                own.step(tt(v4(tmp[:, 0, :]), v4(ps[:, 5 + c % 2, :]), gcol(4, c), ALU.subtract))
                own.step(ts(tmp[:, 1, :], tmp[:, 0, :], 0.0, None, ALU.max))
                ts(tmp[:, 0, :], tmp[:, 0, :], 0.0, None, ALU.min).then_inc(s["growt"], 1)

            for c in range(T):
                growth(c)
            for j in range(8, QKV):
                conv(j)

            def pool(g):
                ve.wait_ge(s["pz"], g + 1)
                src = poolx[:, g, :]
                for n in range(g + 1):
                    dst = poolpp[:, n % 2, :]
                    own.step(tt(dst[:, 16:16 + S], src[:, 16:16 + S], src[:, 16 - (1 << n):16 + S - (1 << n)], ALU.add))
                    src = dst
                own.step(tt(src[:, 16:32], src[:, 16:32], corr[:, g, :], ALU.mult))
                stt(poolcat[:, g, :], src[:, 16:16 + S], 1.0 / POOLS[g], poolx[:, g, 16:16 + S], ALU.mult, ALU.subtract).then_inc(s["pooled"], 1)

            def norm_qk(i):
                ve.wait_ge(s["rsd"], i + 1)
                own.step(nc.vector.reciprocal(rn[:, i % 2, :], rn[:, i % 2, :]))
                stt(qkvT[:, i, :], rn[:, i % 2, :], P ** -0.5 if i < H else 1.0, qkvT[:, i, :], ALU.mult, ALU.mult).then_inc(s["rnorm"], 1)

            ve.wait_ge(s["pzero"], 2)
            for i in range(8):
                norm_qk(i)
                if i >= 4:
                    pool(i - 4)
            ve.wait_ge(s["msum"], 1)
            own.step(tt(modc[:, :, :].rearrange("p v k -> p (v k)"), ps[:, 0, 64:64 + 4 * KD], vec("ada"), ALU.add))
            stt(modc[:, 1, :], modc[:, 1, :], 1.0, vec("g0"), ALU.add, ALU.mult)
            stt(modc[:, 3, :], modc[:, 3, :], 1.0, vec("g2"), ALU.add, ALU.mult).then_inc(s["mod"], 1)
            for n in range(2 * T):
                c = n % T
                ve.wait_ge(s["ktok"], n + 1)
                src = v4(ps[:, c, :])
                if n < T:
                    tt(kbe[:, c], src, gcol(10, c), ALU.mult).then_inc(s["ktoks"], 1)
                    tt(kdec[:, c], src, gcol(8, c), ALU.mult).then_inc(s["ktoks"], 1)
                else:
                    tt(vb[:, c], src, gcol(0, c), ALU.mult).then_inc(s["ktoks"], 1)
            for c in range(T):
                ve.wait_ge(s["masked"], 2 * c + 2)
                ve.wait_ge(s["attn"], c + 1)
                tt(duT[:, c], duT[:, c], v4(ps[:, 4 + c, :]), ALU.mult)
                ve.wait_ge(s["growe"], T)
                tt(qkvT[:, 0:H, c * P:(c + 1) * P], qkvT[:, 0:H, c * P:(c + 1) * P], egr[:, c], ALU.mult).then_inc(s["qd"], 1)
                ve.wait_ge(s["kk"], c + 1)
                tt(Am[:, c], Am[:, c], v4(ps[:, c, :]), ALU.mult).then_inc(s["amat"], 1)
            ident4 = ident.rearrange("p (o n) -> p o n", o=1).broadcast_to([P, H, P])
            ve.wait_ge(s["qd"], T)
            for c in range(T):
                ve.wait_ge(s["bl"], c + 1)
                tt(Tm[:, c], ident4, Bm[:, c], ALU.subtract)
                ve.wait_ge(s["inv0"], c + 1)
                tt(Rm[:, c], ident4, v4(ps[:, 4 + c, :]), ALU.subtract).then_inc(s["upd"], 1)
            for lv in range(1, LEVELS):
                for c in range(T):
                    ve.wait_ge(s["rt"], T * (lv - 1) + c + 1)
                    ve.wait_ge(s["upd"], T * (lv - 1) + c + 1)
                    if lv < LEVELS - 1:
                        tt(Tm[:, c], Tm[:, c], v4(ps[:, 4 + c, :]), ALU.subtract)
                    tt(Rm[:, c], Rm[:, c], v4(ps[:, c, :]), ALU.subtract).then_inc(s["upd"], 1)

            for c in range(T):
                if c < T - 1:
                    ve.wait_ge(s["sup"], c + 1)
                    for h in range(H):
                        src = ps[:, 5, h * P:(h + 1) * P]
                        if c == 0:
                            ins = nc.vector.tensor_copy(state[:, 0, h, :], src)
                        else:
                            if h == 0:
                                ve.wait_ge(s["state"], c)
                                ve.wait_ge(s["o"], c)
                            ins = stt(state[:, c % 2, h, :], state[:, (c - 1) % 2, h, :], gates[:, 7, c * H + h:c * H + h + 1], src, ALU.mult, ALU.add)
                    ins.then_inc(s["state"], 1)
            ve.wait_ge(s["silz"], 1)
            for h in range(H):
                ve.wait_ge(s["ord"], h + 1)
                own.step(nc.vector.reciprocal(orms[:, h, :], orms[:, h, :]))
                own.step(stt(ocat[:, h, :], ocat[:, h, :], vec("dn"), orms[:, h, :], ALU.mult, ALU.mult))
                tt(ocat[:, h, :], ocat[:, h, :], zT[:, h, :], ALU.mult).then_inc(s["onorm"], 1)
            for n in range(N_OUT):
                for t in range(T):
                    ve.wait_ge(s["wout"], n * T + t + 1)
                    tt(x[:, t, n * HALF:(n + 1) * HALF], x[:, t, n * HALF:(n + 1) * HALF], ps[:, n * 4 + t, :], ALU.add).then_inc(s["xa"], 1)

            ve.wait_ge(s["xa"], 2 * T)
            rstd(1)
            ve.wait_ge(s["prow"], 16)
            for t in range(T):
                stt(xn[:, t, :], x[:, t, :], stat[:, 1, t:t + 1], prow[:, 0, :], ALU.mult, ALU.mult).then_inc(s["xs"], 1)
            for kd in range(KD):
                ve.wait_ge(s["qh_hi"], kd + 1)
                tt(a_lo[:, kd, :], ps[:, kd, :], a_hi[:, kd, :], ALU.subtract).then_inc(s["qh_lo"], 1)
            own.step(nc.vector.memset(score[:, T * PH], 0.0))

            def gate_row(m):
                ve.wait_ge(s["gsum"], m + 1)
                lo = slice(m % 2 * HALF, (m % 2 + 1) * HALF)
                own.step(tt(gacc[:, m, :], ps[:, 4 + m, :], rows[:, 2 + m // 2, lo], ALU.add))
                tt(gacc[:, m, :], gacc[:, m, :], rows[:, m // 2, lo], ALU.mult).then_inc(s["gates_out"], 1)

            ve.wait_ge(s["rows"], 16)
            for m in range(N_GATE):
                gate_row(m)
            sflat = score[:, 0:T * PH].rearrange("p (t h) s n -> p t (h s) n", t=T)
            for j in range(2 * PH):
                ve.wait_ge(s["sc"], j + 1)
                nc.vector.tensor_copy(sflat[:, :, j, :], ps[:, 2 + j % 2, :].rearrange("p (t n) -> p t n", t=T)).then_inc(s["scs"], 1)
            dots = sel[:, 1000:1008]
            sexp = lambda par: sel[:, 1024 + 16 * par:1040 + 16 * par]
            ssum = lambda par: sel[:, 1056 + par:1057 + par]
            gate = lambda par: sel[:, 1060 + 16 * par:1076 + 16 * par]
            nmax = lambda par: sel[:, 1100 + par:1101 + par]
            tops = lambda par: sel[:, 1104 + 16 * par:1120 + 16 * par]
            rsum = sel[:, 1136:1137]
            scur = sel[:, 0:256].rearrange("p (s n) -> p s n", s=2)
            top1 = sel[:, 256:288].rearrange("p (s n) -> p s n", s=2)
            fidx = sel[:, 288:320].rearrange("p (s n) -> p s n", s=2)
            cand = sel[:, 320:576]
            onehot = sel[:, 576:832].rearrange("p (k a) -> p k a", a=16)
            fpos = sel[:, 832:848]
            fhi = sel[:, 848:864]
            fpick = sel[:, 864:896].rearrange("p (s n) -> p s n", s=2)
            flo = sel[:, 896:912]
            uidx = selu[:, 32:64].rearrange("p (s n) -> p s n", s=2)
            upos = selu[:, 64:80]
            uhl = selu[:, 80:112].rearrange("p (s n) -> p s n", s=2)

            turn, steps = Own(ve, s["turn"]), own

            def select(i, par, own):
                own.step(nc.vector.tensor_copy(scur, score[:, i] if own is steps else score[:, bass.ds(i, 1)].rearrange("p o s n -> p (o s) n")))
                for hf in range(2):
                    for r in range(2):
                        v8, i8 = top1[:, hf, 8 * r:8 * r + 8], uidx[:, hf, 8 * r:8 * r + 8]
                        own.step(nc.vector.max(v8, scur[:, hf, :]))
                        own.step(nc.vector.max_index(i8, v8, scur[:, hf, :]))
                        if r == 0:
                            own.step(nc.vector.match_replace(scur[:, hf, :], v8, scur[:, hf, :], -3.0e38))
                nc.vector.tensor_copy(fidx, uidx)
                own.step(tt(cand.rearrange("p (a b) -> p a b", b=16), top1[:, 0, :].rearrange("p (a o) -> p a o", o=1).broadcast_to([P, 16, 16]),
                        top1[:, 1, :].rearrange("p (o b) -> p o b", o=1).broadcast_to([P, 16, 16]), ALU.add))
                for r in range(2):
                    v8 = tops(par)[:, 8 * r:8 * r + 8]
                    own.step(nc.vector.max(v8, cand))
                    own.step(nc.vector.max_index(upos[:, 8 * r:8 * r + 8], v8, cand))
                    if r == 0:
                        own.step(nc.vector.match_replace(cand, v8, cand, -3.0e38))
                ts(nmax(par), tops(par)[:, 0:1], -1.0, None, ALU.mult).then_inc(s["smx"], 1)
                ts(uhl[:, 0, :], upos, 4, None, ALU.logical_shift_right)
                own.step(ts(uhl[:, 1, :], upos, 15, None, ALU.bitwise_and))
                nc.vector.tensor_copy(fhi, uhl[:, 0, :])
                own.step(nc.vector.tensor_copy(flo, uhl[:, 1, :]))
                for hf, f in ((0, fhi), (1, flo)):
                    own.step(tt(onehot, f.rearrange("p (k o) -> p k o", o=1).broadcast_to([P, 16, 16]),
                            iota16.rearrange("p (o a) -> p o a", o=1).broadcast_to([P, 16, 16]), ALU.is_equal))
                    own.step(tt(onehot, onehot, fidx[:, hf, :].rearrange("p (o a) -> p o a", o=1).broadcast_to([P, 16, 16]), ALU.mult))
                    own.step(nc.vector.tensor_reduce(fpick[:, hf, :], onehot, AX.X, ALU.add))
                own.step(stt(fpos, fpick[:, 0, :], float(NK), fpick[:, 1, :], ALU.mult, ALU.add))
                nc.vector.tensor_copy(selu[:, par * 16:par * 16 + 16], fpos).then_inc(s["idx"], 1)

            def finish(n, par, own):
                ve.wait_ge(s["sexp"], n)
                own.step(nc.vector.reciprocal(rsum, ssum(par)))
                ts(gate(par), sexp(par), rsum, None, ALU.mult).then_inc(s["gate"], 1)

            select(0, 0, steps)
            finish(1, 0, steps)
            with ve.Fori(0, T) as t:
                turn.n = 0
                turn.step(nc.vector.tensor_copy(xcur, xn[:, bass.ds(t, 1), :].rearrange("p o n -> p (o n)")))
                ve.sem_clear(s["turn"])
                with ve.Fori(0, PH // 2) as hp:
                    it = t * (PH // 2) + hp
                    turn.n = 0
                    for b in range(2 * TOPK // BATCH):
                        k0 = b * BATCH
                        for k in range(k0, k0 + BATCH):
                            r = ring[k % GRING]
                            ve.wait_ge(gathered[k % GRING], it * 64 + 16 * (k // GRING + 1))
                            ins = nc.vector.tensor_tensor_reduce(r[:, 0:D], r[:, 0:D], xcur, 1.0, 0.0, ALU.mult, ALU.add,
                                                                 dots[:, b % 2 * 4 + k % 4:b % 2 * 4 + k % 4 + 1])
                        ins.then_inc(s["dots"], 1)
                        if b % 4 == 2:
                            par = 1 - b // 4
                            select(it * 2 + (2 if par == 0 else 1), par, turn)
                        if b % 4 == 3:
                            par = 1 - b // 4
                            finish(it * 2 + (3 if par == 0 else 2), par, turn)
                    ve.sem_clear(s["turn"])

            rstd(2)
            ve.wait_ge(s["acc_out"], T)
            for t in range(T):
                stt(x[:, t, :], x[:, t, :], stat[:, 1, t:t + 1], prow[:, 1, :], ALU.mult, ALU.mult).then_inc(s["seln"], 1)
            rstd(3)
            ve.wait_ge(s["seln"], T)
            for t in range(T):
                ts(xs2[:, t, :], x[:, t, :], stat[:, 1, t:t + 1], None, ALU.mult).then_inc(s["xs"], 1)

            def split_hT(k):
                for kd in range(KD):
                    ve.wait_ge(s["a_y"], KD * k + kd + 1)
                    nc.vector.tensor_copy(a_hi[:, kd, :], y_hT[:, kd, :]).then_inc(s["a_hi"], 1)
                    ve.wait_ge(s["a_hi"], KD * k + kd + 1)
                    tt(a_lo[:, kd, :], y_hT[:, kd, :], a_hi[:, kd, :], ALU.subtract).then_inc(s["a_lo"], 1)

            split_hT(0)
            ve.wait_ge(s["zero"], 2)
            for m in range(1, 24, 2):
                ve.wait_ge(s["unit_used"], m + 1 if m < 16 else m // 4 * 4 + 4)
                if m < 8:
                    ts(qz[0:64, 2 * m, :], ps[0:64, m % 8, :], 0.125, None, ALU.mult)
                    ts(qz[64:128, 2 * m + 1, :], ps[64:128, m % 8, :], 0.125, None, ALU.mult).then_inc(s["qkv_d"], 1)
                elif m < 16:
                    nc.vector.tensor_copy(kT2[:, m - 8, :], ps[:, m % 8, :]).then_inc(s["qkv_d"], 1)
                else:
                    nc.vector.tensor_copy(v2[:, m % 4, (m - 16) // 4 * HALF:((m - 16) // 4 + 1) * HALF], ps[:, m % 8, :]).then_inc(s["qkv_d"], 1)

            def out_lo(i):
                ve.wait_ge(s["o_hi"], i + 1)
                tt(a_lo[:, i, :], ps[:, 6 + i % 2, :], a_hi[:, i, :], ALU.subtract).then_inc(s["o_lo"], 1)

            for h in range(AH):
                zz = psf[:, h % 2 * 1536:h % 2 * 1536 + ZW]
                ve.wait_ge(s["lnp"], 3 * h + 3)
                stt(spb[h % 3], zz, 0.0, spb[h % 3], ALU.max, ALU.add).then_inc(s["spd"], 1)
                ve.wait_ge(s["spd"], h + 1)
                if h >= 1:
                    ve.wait_ge(s["rest"], h)
                nc.vector.tensor_copy(sp_hi, spb[h % 3]).then_inc(s["sp_hi"], 1)
                ve.wait_ge(s["sp_hi"], h + 1)
                tt(sp_lo, spb[h % 3], sp_hi, ALU.subtract).then_inc(s["sp_lo"], 1)
                if h % 2 == 0 and h >= 4:
                    out_lo(h // 2 - 2)
            out_lo(AH // 2 - 2)
            out_lo(AH // 2 - 1)

            def branch(k):
                ve.wait_ge(s["ysq"], (T + 1) * (k + 1))
                own.step(nc.vector.reciprocal(stat[:, 3, :], stat[:, 3, :]))
                for t in range(T):
                    y = ps[:, 2 * t:2 * t + 2, :].rearrange("p b n -> p (b n)")
                    own.step(stt(tail[:, t % 2, :], y, stat[:, 3, t:t + 1], gtrow[:, k, :], ALU.mult, ALU.mult))
                    tt(x[:, t, :], x[:, t, :], tail[:, t % 2, :], ALU.add).then_inc(s["yfree" if k == 0 else "fin"], 1)

            ve.wait_ge(s["y"], T)
            branch(0)
            rstd(4)
            ve.wait_ge(s["yfree"], T)
            for t in range(T):
                ts(xs2[:, t, :], x[:, t, :], stat[:, 1, t:t + 1], None, ALU.mult).then_inc(s["xs"], 1)
            split_hT(1)
            for j in range(FT):
                ve.wait_ge(s["ffs"], j + 1)
                own.step(tt(ff[:, j % 2, :], ff[:, j % 2, :], ps[:, 2 * j % 8 + 1, :], ALU.mult))
                own.step(nc.vector.tensor_copy(act_hi[:, j, :], ff[:, j % 2, :]))
                tt(act_lo[:, j, :], ff[:, j % 2, :], act_hi[:, j, :], ALU.subtract).then_inc(s["ffd"], 1)
            ve.wait_ge(s["y"], 2 * T)
            branch(1)


def laid_out(inputs):
    g = {k: np.asarray(v) for k, v in inputs.items()}

    def cols(v):
        return v.reshape(-1, P).T

    def chunks(w):
        return w.reshape(KD, P, -1, HALF).transpose(2, 1, 0, 3)

    DN = H * P
    w_in = g["w_in"][0]
    heads = w_in[:, 0:3 * DN], w_in[:, 4 * DN + 2 * H:], w_in[:, 3 * DN:4 * DN]
    early = [chunks(np.concatenate(heads, axis=1)), chunks(g["w_out"][0]), chunks(g["w_query"][0])]
    fin = g["ffn_w_in_2"][0]
    fin = np.stack([fin[:, :FF].reshape(D, -1, 256), fin[:, FF:].reshape(D, -1, 256)], axis=2).reshape(D, -1)
    fout = g["ffn_w_out_2"][0].reshape(FT, P, D)
    fout = np.concatenate([fout, np.zeros((-FT % 4, P, D), fout.dtype)])
    fout = fout.reshape(-1, 4, P, D).transpose(0, 2, 1, 3).reshape(-1, P, KD, HALF)
    late = [chunks(g["sb_w_qkv_2"][0]), chunks(g["sb_w_o_2"][0]), chunks(fin), fout]
    adab = g["ada_b_2"][0].reshape(6, D)
    adaw = g["ada_w_2"][0].reshape(D, 6, D)[:, [0, 1, 3, 4, 2, 5]].reshape(D, 6 * D)
    ng = g["norm_g_2"][0]
    parts = {
        "norm_mix": cols(g["norm_mix_w"][0]),
        "conv": g["conv_w"][0].reshape(CW, QKV, P).transpose(2, 1, 0).reshape(P, -1),
        "dn": g["dn_norm_w"][0][:, None],
        "pool": cols(g["pool_scale"][0]),
        "g0": cols(ng[0]), "g2": cols(ng[2]), "c": cols(g["c_2"][0]),
        "ada": np.concatenate([cols(adab[n]) for n in (0, 1, 3, 4)], axis=1),
        "alog": np.broadcast_to(g["a_log"][0], (P, H)), "dtb": np.broadcast_to(g["dt_bias"][0], (P, H)),
    }
    consts, levels = shape_constants()
    arrays = {
        "x": g["x"][0], "consts": consts, "levels": levels,
        "vecs": np.concatenate([parts[n] for n in VEC], axis=1),
        "w_ba": w_in[:, 4 * DN:4 * DN + 2 * H].reshape(KD, P, 2 * H).transpose(1, 0, 2),
        "w_pool": g["w_pool"][0].transpose(1, 0, 2),
        "rows": np.stack([ng[1], ng[3], adab[2], adab[5]]),
        "prow": np.stack([g["norm_ffn_w"][0], g["norm_final_w"]]),
        "sub_keys": g["sub_keys"][0].reshape(2 * PH, NK, P).transpose(2, 0, 1),
        "w_early": np.concatenate(early), "w_late": np.concatenate(late), "w_ada": chunks(adaw),
        "experts": np.concatenate([g["expert_down"][0], g["expert_up"][0]], axis=1),
    }
    return {f"in_{k}": np.ascontiguousarray(v) for k, v in arrays.items()}


def kernel(**inputs):
    import concourse.bacc as _bacc
    from concourse.bass_utils import run_bass_kernel_spmd as _run

    nc = _bacc.Bacc("TRN2", target_bir_lowering=False, num_devices=1)
    arrays = laid_out(inputs)
    aps = {k[3:]: nc.dram_tensor(k, v.shape, mybir.dt.from_np(v.dtype), kind="ExternalInput").ap() for k, v in arrays.items()}
    out = nc.dram_tensor("out_dram", (1, S, D), F32, kind="ExternalOutput").ap()
    block_kernel(nc, aps, out)
    r = _run(nc, [arrays], core_ids=[0])
    return r.results[0]["out_dram"]
```
